# Optimizing a Trainium2 kernel written in Bass

```python
import jax, jax.numpy as jnp
from jax import lax
import numpy as np

D_MODEL = 1024
BATCH = 1
SEQ = 512
DEPTH = 2

N_MIXERS = 2
CONV_CH = D_MODEL
CONV_KERNEL = 31
GMLP_CHUNK = 128
GMLP_GROUPS = 8
GMLP_DFF = 2 * D_MODEL
GMLP_HALF = GMLP_DFF // 2
GMLP_GROUP_CH = GMLP_HALF // GMLP_GROUPS
FFN_HIDDEN = 2816
FFN_CONV = 3
DEEPNORM_ALPHA = (2.0 * DEPTH) ** 0.25
DEEPNORM_BETA = (8.0 * DEPTH) ** -0.25
LN_EPS = 1e-5
N_CONV_LAYERS = (DEPTH + 1) // 2
N_GMLP_LAYERS = DEPTH // 2

kernel_name = "hybrid_conformer_gmlp_deepnorm"

def layer_norm(x, g, b):
    xf = x.astype(jnp.float32)
    mu = jnp.mean(xf, axis=-1, keepdims=True)
    xc = xf - mu
    var = jnp.mean(xc * xc, axis=-1, keepdims=True)
    y = xc * lax.rsqrt(var + LN_EPS)
    return (y * g.astype(jnp.float32) + b.astype(jnp.float32)).astype(x.dtype)

def causal_depthwise_conv(x, w, b):
    k, c = w.shape
    y = lax.conv_general_dilated(
        x, w[:, None, :].astype(x.dtype), window_strides=(1,), padding=[(k - 1, 0)],
        dimension_numbers=("NWC", "WIO", "NWC"), feature_group_count=c)
    return y + b

def conformer_conv_module(x, w_in, b_in, w_dw, b_dw, ln_g, ln_b, w_out, b_out):
    h = x @ w_in + b_in
    a, gate = jnp.split(h, 2, axis=-1)
    h = a * jax.nn.sigmoid(gate)
    h = causal_depthwise_conv(h, w_dw, b_dw)
    h = jax.nn.silu(layer_norm(h, ln_g, ln_b))
    return h @ w_out + b_out

def chunked_spatial_gating(x, w_in, b_in, ln_g, ln_b, w_s, b_s, w_out, b_out):
    bsz, t, _ = x.shape
    z = jax.nn.gelu(x @ w_in + b_in, approximate=False)
    u, v = jnp.split(z, 2, axis=-1)
    v = layer_norm(v, ln_g, ln_b)
    n_chunks = t // GMLP_CHUNK
    v = v.reshape(bsz, n_chunks, GMLP_CHUNK, GMLP_GROUPS, GMLP_GROUP_CH)
    mask = jnp.tril(jnp.ones((GMLP_CHUNK, GMLP_CHUNK), dtype=bool))
    w_causal = jnp.where(mask[None], w_s, jnp.zeros((), w_s.dtype))
    s = jnp.einsum("gts,bnsgc->bntgc", w_causal, v) + b_s.T[:, :, None]
    s = s.reshape(bsz, t, GMLP_HALF)
    return (u * s) @ w_out + b_out

def conv_ffn(x, w_up, b_up, w_dw, b_dw, w_down, b_down):
    h = x @ w_up + b_up
    h = causal_depthwise_conv(h, w_dw, b_dw)
    g, val = jnp.split(h, 2, axis=-1)
    return (jax.nn.silu(g) * val) @ w_down + b_down

def setup_inputs(seed: int = 0) -> dict:
    key = jax.random.key(seed)
    ks = iter(jax.random.split(key, 32))

    def nrm(shape, std):
        return jax.random.normal(next(ks), shape, jnp.float32) * std

    def xavier_out(shape):
        fan_in, fan_out = shape[-2], shape[-1]
        return nrm(shape, DEEPNORM_BETA * (2.0 / (fan_in + fan_out)) ** 0.5)

    na, nb, d = N_CONV_LAYERS, N_GMLP_LAYERS, D_MODEL
    inp = {}
    inp["x"] = nrm((BATCH, SEQ, d), 1.0)
    inp["conv_w_in"] = nrm((na, d, 2 * CONV_CH), d ** -0.5)
    inp["conv_b_in"] = nrm((na, 2 * CONV_CH), 0.02)
    inp["conv_w_dw"] = nrm((na, CONV_KERNEL, CONV_CH), CONV_KERNEL ** -0.5)
    inp["conv_b_dw"] = nrm((na, CONV_CH), 0.02)
    inp["conv_ln_g"] = 1.0 + nrm((na, CONV_CH), 0.05)
    inp["conv_ln_b"] = nrm((na, CONV_CH), 0.02)
    inp["conv_w_out"] = xavier_out((na, CONV_CH, d))
    inp["conv_b_out"] = nrm((na, d), 0.02)
    inp["gmlp_w_in"] = nrm((nb, d, GMLP_DFF), d ** -0.5)
    inp["gmlp_b_in"] = nrm((nb, GMLP_DFF), 0.02)
    inp["gmlp_ln_g"] = 1.0 + nrm((nb, GMLP_HALF), 0.05)
    inp["gmlp_ln_b"] = nrm((nb, GMLP_HALF), 0.02)
    inp["gmlp_w_s"] = nrm((nb, GMLP_GROUPS, GMLP_CHUNK, GMLP_CHUNK), 0.5 * GMLP_CHUNK ** -0.5)
    inp["gmlp_b_s"] = 1.0 + nrm((nb, GMLP_GROUPS, GMLP_CHUNK), 0.1)
    inp["gmlp_w_out"] = xavier_out((nb, GMLP_HALF, d))
    inp["gmlp_b_out"] = nrm((nb, d), 0.02)
    inp["ffn_w_up"] = nrm((DEPTH, d, 2 * FFN_HIDDEN), d ** -0.5)
    inp["ffn_b_up"] = nrm((DEPTH, 2 * FFN_HIDDEN), 0.02)
    inp["ffn_w_dw"] = nrm((DEPTH, FFN_CONV, 2 * FFN_HIDDEN), FFN_CONV ** -0.5)
    inp["ffn_b_dw"] = nrm((DEPTH, 2 * FFN_HIDDEN), 0.02)
    inp["ffn_w_down"] = xavier_out((DEPTH, FFN_HIDDEN, d))
    inp["ffn_b_down"] = nrm((DEPTH, d), 0.02)
    inp["norm1_g"] = 1.0 + nrm((DEPTH, d), 0.05)
    inp["norm1_b"] = nrm((DEPTH, d), 0.02)
    inp["norm2_g"] = 1.0 + nrm((DEPTH, d), 0.05)
    inp["norm2_b"] = nrm((DEPTH, d), 0.02)
    return inp

def reference(x, conv_w_in, conv_b_in, conv_w_dw, conv_b_dw, conv_ln_g, conv_ln_b,
              conv_w_out, conv_b_out, gmlp_w_in, gmlp_b_in, gmlp_ln_g, gmlp_ln_b,
              gmlp_w_s, gmlp_b_s, gmlp_w_out, gmlp_b_out, ffn_w_up, ffn_b_up,
              ffn_w_dw, ffn_b_dw, ffn_w_down, ffn_b_down, norm1_g, norm1_b,
              norm2_g, norm2_b):
    for i in range(DEPTH):
        j = i // N_MIXERS
        if i % N_MIXERS == 0:
            y = conformer_conv_module(x, conv_w_in[j], conv_b_in[j], conv_w_dw[j], conv_b_dw[j],
                                      conv_ln_g[j], conv_ln_b[j], conv_w_out[j], conv_b_out[j])
        else:
            y = chunked_spatial_gating(x, gmlp_w_in[j], gmlp_b_in[j], gmlp_ln_g[j], gmlp_ln_b[j],
                                       gmlp_w_s[j], gmlp_b_s[j], gmlp_w_out[j], gmlp_b_out[j])
        x = layer_norm(DEEPNORM_ALPHA * x + y, norm1_g[i], norm1_b[i])
        y = conv_ffn(x, ffn_w_up[i], ffn_b_up[i], ffn_w_dw[i], ffn_b_dw[i],
                     ffn_w_down[i], ffn_b_down[i])
        x = layer_norm(DEEPNORM_ALPHA * x + y, norm2_g[i], norm2_b[i])
    return x


_drawn_inputs = setup_inputs


def setup_inputs(seed=0):
    import zlib

    import numpy as np

    out = dict(_drawn_inputs(seed))
    spreads = {}
    factors = {'conv_b_in': 8.0,
     'conv_b_dw': 6.127,
     'conv_ln_g': 4.127,
     'conv_ln_b': 8.0,
     'conv_b_out': 4.019,
     'gmlp_b_in': 8.0,
     'gmlp_ln_g': 8.0,
     'gmlp_ln_b': 42.643,
     'gmlp_b_out': 4.05,
     'ffn_b_up': 5.427,
     'ffn_b_dw': 5.555,
     'ffn_b_down': 2.798,
     'gmlp_b_s': 2.877}
    for name, (base, spread) in spreads.items():
        noise = np.random.default_rng([zlib.crc32(name.encode()), seed]).standard_normal(out[name].shape)
        drawn = base * np.exp(spread * noise) if base else spread * noise
        out[name] = __import__('jax').numpy.asarray(drawn.astype(out[name].dtype))
    for name, factor in factors.items():
        out[name] = (out[name] * factor).astype(out[name].dtype)
    return out
```

```python
import concourse.bass as bass
from concourse import mybir

P = 128
D = 1024
SEQ = 512
DEPTH = 2
NT = SEQ // P
KD = D // P
HID = 2816
KH = HID // P
HALF = 512
TAPS = 31
PAD = TAPS - 1
FTAPS = 3
FPAD = FTAPS - 1
GROUPS = 8
ALPHA = (2.0 * DEPTH) ** 0.25
EPS = 1e-5
UNIT = 1024

U_CONV_IN = 0
U_CONV_OUT = U_CONV_IN + 2 * KD
U_UP0 = U_CONV_OUT + KD
U_DOWN0 = U_UP0 + 2 * KH
U_GV = U_DOWN0 + KH
U_GU = U_GV + KD
U_GOUT = U_GU + KD
U_UP1 = U_GOUT + KD
U_DOWN1 = U_UP1 + 2 * KH
UNITS = U_DOWN1 + KH

RAW = 4
RING = 4
LEAD = 3

PE_TAPS = 11
DV_TAPS = TAPS - PE_TAPS

C_CIN_B = 0
C_CDW_W = C_CIN_B + 2 * KD
C_CDW_B = C_CDW_W + KD * TAPS
C_CLN_G = C_CDW_B + KD
C_CLN_B = C_CLN_G + KD
C_GU_B = C_CLN_B + KD
C_FUP_B = C_GU_B + KD
C_FDW_W = C_FUP_B + DEPTH * KH * 2
C_FDW_B = C_FDW_W + DEPTH * KH * 2 * FTAPS
NPAR = C_FDW_B + DEPTH * KH * 2

(R_N1G, R_N1B, R_N2G, R_N2B, R_N3G, R_N3B, R_N4G, R_N4B, R_BO1, R_BO2, R_BO3, R_BO4,
 R_GVB, R_GLG, R_GLB, R_GBS, NROW) = range(17)


def build_trunk(nc, x_tm_d, x_fm_d, weights_d, params_d, rows_d, spatial_d, out_d):
    f32 = mybir.dt.float32
    f32r = mybir.dt.float32r
    ALU = mybir.AluOpType
    ACT = mybir.ActivationFunctionType

    base = (nc.sbuf_base + 63) // 64 * 64
    at = [base]

    def place(name, shape, dt, offset=None):
        size = 4
        for n in shape[1:]:
            size *= n
        if offset is None:
            offset = at[0]
            at[0] += (size + 31) // 32 * 32
        return nc.alloc_sbuf_tensor_at(name, shape, dt, offset=offset)

    raw = place("raw", [P, RAW, UNIT], f32)
    wh = place("wh", [P, RING, UNIT], f32r)
    wl = place("wl", [P, RING, UNIT], f32r)
    xh = place("xh", [P, KD, SEQ], f32r)
    xl = place("xl", [P, KD, SEQ], f32r)
    res = place("res", [P, NT, D], f32)
    par = place("par", [P, NPAR], f32)
    brow = place("brow", [P, D], f32)
    ident = place("ident", [P, P], f32)
    half_m = place("half_m", [P, NT], f32)
    stats = place("stats", [P, NT, 2, 6], f32)
    mv = place("mv", [P, NT, 2], f32)
    veps = place("veps", [P, NT], f32)
    rstd = place("rstd", [P, NT], f32)

    s0 = at[0]
    at[0] += 2 * 2080 + 4 * 2048
    grow = place("grow", [P, D], f32, s0)
    brow_n = place("brow_n", [P, D], f32, s0 + 4096)
    bsrow = place("bsrow", [P, GROUPS, P], f32, s0 + 8192)
    gpad = place("gpad", [P, FPAD + SEQ], f32, s0)
    vpad = place("vpad", [P, FPAD + SEQ], f32, s0 + 2080)
    gacc = place("gacc", [P, SEQ], f32, s0 + 4160)
    vacc = place("vacc", [P, SEQ], f32, s0 + 4160 + 2048)
    prod = place("prod", [P, SEQ], f32, s0 + 4160 + 4096)

    h0 = at[0]
    hh = place("hh", [P, KH, SEQ], f32r)
    hl = place("hl", [P, KH, SEQ], f32r)
    assert at[0] <= nc.sbuf_usable_end, (at[0], nc.sbuf_usable_end)
    hend = at[0]
    at[0] = h0
    CW = PAD + SEQ
    xraw = place("xraw", [P, KD, SEQ], f32)
    glu = place("glu", [P, 2, CW], f32)
    gluh = place("gluh", [P, 2, CW], f32r)
    glul = place("glul", [P, 2, CW], f32r)
    sig = place("sig", [P, SEQ], f32)
    acc = place("acc", [P, 2, SEQ], f32)
    cbuf = place("cbuf", [P, 2, SEQ], f32)
    dwl = place("dwl", [P, KD * TAPS], f32)
    dwh = place("dwh", [P, KD * TAPS], f32r)
    diagh = place("diagh", [P, 2, PE_TAPS, P], f32r)
    diagl = place("diagl", [P, 2, PE_TAPS, P], f32r)
    ctm = place("ctm", [P, NT, D], f32)
    slb = place("slb", [P, 2, SEQ], f32)
    assert at[0] <= hend
    vtm = place("vtm", [P, NT, D], f32, h0)
    ush = place("ush", [P, KD, SEQ], f32r, h0 + 16384)
    usl = place("usl", [P, KD, SEQ], f32r, h0)
    gvrow = place("gvrow", [P, D], f32, h0 + 16384)
    glg = place("glg", [P, D], f32, h0 + 16384 + 4096)
    glb = place("glb", [P, D], f32, h0 + 16384 + 8192)
    wsraw = place("wsraw", [P, GROUPS, P], f32, h0 + 16384 + 12288)
    vh = place("vh", [P, NT, D], f32r, h0 + 32768)
    vl = place("vl", [P, NT, D], f32r, h0 + 49152)
    uu = place("uu", [P, KD, SEQ], f32, h0 + 65536)
    wsh = place("wsh", [P, GROUPS, P], f32r, h0 + 81920)
    wsl = place("wsl", [P, GROUPS, P], f32r, h0 + 81920 + 4096)

    ps = nc.alloc_psum_tensor("ps", [P, 8, 512], f32)

    sem = nc.alloc_semaphore
    raw_in = [sem(f"raw_in{i}") for i in range(RAW)]
    xfm_in = [sem(f"xfm_in{i}") for i in range(4)]
    xtm_in = sem("xtm_in")
    par_in = sem("par_in")
    bo_in = sem("bo_in")
    norm_in = sem("norm_in")
    gm_in = sem("gm_in")
    out_done = sem("out_done")
    const_ok = sem("const_ok")
    w_hi = sem("w_hi")
    w_lo = sem("w_lo")
    w_used = sem("w_used")
    x_hi = sem("x_hi")
    x_lo = sem("x_lo")
    res_ok = sem("res_ok")
    res_mul = sem("res_mul")
    dw_ok = sem("dw_ok")
    diag = sem("diag")
    gate_s = sem("gate_s")
    glu_s = sem("glu_s")
    glu_hi = sem("glu_hi")
    glu_lo = sem("glu_lo")
    dw_pe = sem("dw_pe")
    dw_tap = sem("dw_tap")
    conv_c = sem("conv_c")
    ct_pe = sem("ct_pe")
    ct_ok = sem("ct_ok")
    zc = sem("zc")
    zt = sem("zt")
    sl = sem("sl")
    blk = sem("blk")
    st_ok = sem("st_ok")
    var_ok = sem("var_ok")
    eps_ok = sem("eps_ok")
    rstd_ok = sem("rstd_ok")
    nrm = sem("nrm")
    x_ok = sem("x_ok")
    xt = sem("xt")
    g_in = sem("g_in")
    v_in = sem("v_in")
    tap = sem("tap")
    PAD_TAPS = 2 * 2 * FTAPS
    gs = sem("gs")
    pr = sem("pr")
    h_hi = sem("h_hi")
    h_lo = sem("h_lo")
    v_ev = sem("v_ev")
    v_gelu = sem("v_gelu")
    u_gelu = sem("u_gelu")
    v_n = sem("v_n")
    v_hi = sem("v_hi")
    v_lo = sem("v_lo")
    ws_m = sem("ws_m")
    ws_hi = sem("ws_hi")
    ws_lo = sem("ws_lo")
    sp = sem("sp")
    sp_b = sem("sp_b")
    us_s = sem("us_s")
    us_hi = sem("us_hi")
    us_lo = sem("us_lo")

    XCH = KD // 2
    X0 = XCH
    XC = X0 + KD
    XN = [XC + 2 * NT * (n + 1) for n in range(3)]
    B0 = [0, 0, 4, 4]
    B1 = [4, 4, 0, 0]

    block = nc.Block()
    block.__enter__()

    @block.sync
    def _(eng):
        def load(slot, unit):
            eng.dma_start(raw[:, slot, :], weights_d[bass.ds(unit, 1), :, :].rearrange("o p n -> p (o n)")
                          ).then_inc(raw_in[slot], 16)

        eng.dma_start(par[:, :], params_d).then_inc(par_in, 16)
        for s in range(RAW):
            load(s, s)
            eng.dma_start(xraw[:, 2 * s:2 * s + 2, :], x_fm_d[:, 2 * s:2 * s + 2, :]).then_inc(xfm_in[s], 16)
        with eng.Fori(1, UNITS // RAW) as i:
            for s in range(RAW):
                eng.wait_ge(w_lo, i * RAW + (s - RAW + 1))
                load(s, i * RAW + s)
        for t in range(NT):
            eng.wait_ge(x_ok, 3 * NT + t + 1)
            eng.dma_start(out_d[t * P:(t + 1) * P, :], res[:, t, :]).then_inc(out_done, 16)
        eng.wait_ge(out_done, 16 * NT)

    @block.gpsimd
    def _(eng):
        def row(dst, r, s):
            eng.dma_start(dst, rows_d[r:r + 1, :].partition_broadcast(P)).then_inc(s, 16)

        def norm_rows(n):
            row(grow[:, :], R_N1G + 2 * n, norm_in)
            row(brow_n[:, :], R_N1B + 2 * n, norm_in)

        def residual(n, t):
            k = n * NT + t
            eng.tensor_scalar(res[:, t, :], res[:, t, :], ALPHA, None, ALU.mult).then_inc(res_mul, 1)
            eng.wait_ge(res_mul, k + 1)
            eng.tensor_tensor(res[:, t, :], res[:, t, :], brow[:, :], ALU.add).then_inc(res_ok, 1)

        def inverse_root(k, t, n):
            eng.wait_ge(var_ok, k + 1)
            eng.tensor_scalar(veps[:, t:t + n], mv[:, t:t + n, 1], EPS, None, ALU.add).then_inc(eps_ok, 1)
            eng.wait_ge(eps_ok, k + 1)
            eng.tensor_tensor(rstd[:, t:t + n], veps[:, t:t + n], half_m[:, t:t + n], ALU.pow).then_inc(rstd_ok, 1)

        row(brow[:, :], R_BO1, bo_in)
        for t in range(NT):
            eng.dma_start(res[:, t, :], x_tm_d[t * P:(t + 1) * P, :]).then_inc(xtm_in, 16)
        norm_rows(0)
        eng.memset(half_m[:, :], -0.5).then_inc(const_ok, 1)
        eng.memset(ident[:, :], 0.0).then_inc(const_ok, 1)
        eng.wait_ge(const_ok, 2)
        eng.affine_select(out=ident[:, :], in_=ident[:, :], compare_op=ALU.not_equal, fill=1.0, base=0,
                          pattern=[[-1, P]], channel_multiplier=1).then_inc(const_ok, 1)
        eng.wait_ge(const_ok, 3)

        def diagonals(j):
            if j == 0:
                eng.wait_ge(dw_ok, 2)
            if j >= 2:
                eng.wait_ge(dw_pe, j - 1)
            eye = ident[:, :].rearrange("p (o n) -> p o n", o=1).broadcast_to([P, PE_TAPS, P])
            c0 = j * TAPS + DV_TAPS
            hi = par[:, C_CDW_W + c0:C_CDW_W + c0 + PE_TAPS].rearrange("p (n o) -> p n o", o=1).broadcast_to([P, PE_TAPS, P])
            lo = dwl[:, c0:c0 + PE_TAPS].rearrange("p (n o) -> p n o", o=1).broadcast_to([P, PE_TAPS, P])
            eng.tensor_tensor(diagh[:, j % 2, :, :], eye, hi, ALU.mult).then_inc(diag, 1)
            eng.tensor_tensor(diagl[:, j % 2, :, :], eye, lo, ALU.mult).then_inc(diag, 1)

        diagonals(0)
        diagonals(1)
        eng.wait_ge(xtm_in, 16 * NT)
        eng.wait_ge(bo_in, 16)
        for j in range(2, KD):
            diagonals(j)
            if j - 2 < NT:
                residual(0, j - 2)
        eng.wait_ge(res_ok, NT)
        row(brow[:, :], R_BO2, bo_in)
        inverse_root(0, 0, NT)
        for n in range(DEPTH * 2):
            for t in range(NT):
                inverse_root(1 + n * NT + t + (NT if n >= 2 else 0), t, 1)
            if n == 3:
                break
            eng.wait_ge(bo_in, 16 * (n + 2))
            for t in range(NT):
                eng.wait_ge(xt, 2 * (n * NT + t + 1))
                residual(n + 1, t)
            if n < 2:
                eng.wait_ge(res_ok, (n + 2) * NT)
                row(brow[:, :], R_BO3 + n, bo_in)
            if n != 1:
                eng.wait_ge(h_lo, KH * (n // 2 + 1))
                norm_rows(n + 1)
            else:
                eng.wait_ge(w_used, U_GV)
                row(gvrow[:, :], R_GVB, gm_in)
                row(glg[:, :], R_GLG, gm_in)
                row(glb[:, :], R_GLB, gm_in)
                eng.dma_start(wsraw[:, :, :], spatial_d).then_inc(gm_in, 16)
                eng.wait_ge(x_ok, 2 * NT)
                row(bsrow[:, :, :].rearrange("p g t -> p (g t)"), R_GBS, gm_in)
                norm_rows(2)
                eng.wait_ge(gm_in, 16 * 5)
                eng.affine_select(out=wsraw[:, :, :], in_=wsraw[:, :, :], compare_op=ALU.is_ge, fill=0.0,
                                  base=0, pattern=[[0, GROUPS], [1, P]], channel_multiplier=-1).then_inc(ws_m, 1)
                for t in range(NT):
                    inverse_root(1 + 2 * NT + t, t, 1)

    @block.scalar
    def _(eng):
        def hi(u):
            eng.wait_ge(raw_in[u % RAW], 16 + u // RAW * 16)
            eng.activation(wh[:, u % RING, :], raw[:, u % RAW, :], ACT.Copy).then_inc(w_hi, 1)

        def his(units):
            for u in units:
                if u >= UNITS:
                    return
                if u >= RING:
                    eng.wait_ge(w_used, u - RING + 1)
                hi(u)

        eng.wait_ge(xfm_in[0], 16)
        eng.activation(xh[:, 0:2, :], xraw[:, 0:2, :], ACT.Copy).then_inc(x_hi, 1)
        his(range(0, 1))
        for c in range(1, XCH):
            eng.wait_ge(xfm_in[c], 16)
            eng.activation(xh[:, 2 * c:2 * c + 2, :], xraw[:, 2 * c:2 * c + 2, :], ACT.Copy).then_inc(x_hi, 1)
        his(range(1, LEAD))
        eng.wait_ge(par_in, 16)

        def ct_out(j):
            eng.wait_ge(ct_pe, j + 1)
            eng.activation(ctm[:, :, j * P:(j + 1) * P],
                           ps[:, 6 + j % 2, :].rearrange("p (t n) -> p t n", t=NT), ACT.Copy).then_inc(ct_ok, 1)

        for j in range(KD):
            his([2 * j + LEAD])
            eng.wait_ge(w_used, 2 * j + 1)
            if j >= 1:
                eng.wait_ge(glu_s, j)
            b = C_CIN_B + KD + j
            eng.activation(sig[:, :], ps[:, 2 * j % 4, :], ACT.Sigmoid, bias=par[:, b:b + 1]).then_inc(gate_s, 1)
            eng.wait_ge(glu_s, j + 1)
            if j >= 2:
                eng.wait_ge(dw_pe, j - 1)
            eng.activation(gluh[:, j % 2, PAD:CW], glu[:, j % 2, PAD:CW], ACT.Copy).then_inc(glu_hi, 1)
            his([2 * j + 1 + LEAD])
            if j >= 2:
                ct_out(j - 2)
        ct_out(KD - 2)
        ct_out(KD - 1)

        ahead = {0: U_CONV_OUT + 3, 3: U_CONV_OUT + 4, 5: U_CONV_OUT + 5, 7: U_CONV_OUT + 6}
        for k in range(KD):
            eng.wait_ge(zt, k + 1)
            if k >= 2:
                eng.wait_ge(x_lo, X0 + k - 1)
            eng.activation(slb[:, k % 2, :], ps[:, 4 + k % 2, :], ACT.Silu, scale=par[:, C_CLN_G + k:C_CLN_G + k + 1],
                           bias=par[:, C_CLN_B + k:C_CLN_B + k + 1]).then_inc(sl, 1)
            eng.wait_ge(sl, k + 1)
            eng.activation(xh[:, k, :], slb[:, k % 2, :], ACT.Copy).then_inc(x_hi, 1)
            if k in ahead:
                his([ahead[k]])
        his([U_CONV_OUT + 7])

        def block_hi(n, t):
            for q in range(2):
                eng.wait_ge(xt, 2 * (n * NT + t) + q + 1)
                eng.activation(xh[:, 4 * q:4 * q + 4, t * P:(t + 1) * P],
                               ps[:, B0[n] + 2 * (t % 2) + q, :].rearrange("p (k n) -> p k n", k=4), ACT.Copy).then_inc(x_hi, 1)

        def norm_hi(n, u_next):
            for t in range(NT - 1):
                block_hi(n, t)
            his([u_next])
            block_hi(n, NT - 1)
            his([u_next + 1, u_next + 2])

        def ffn_up(layer, u0, bank0):
            ring = u0 % RING
            first_tap = PAD_TAPS * (layer + 1) + 6 * KH * layer

            def unit_hi(i, c):
                slot = (ring + c) % RING
                eng.wait_ge(w_used, i * 4 + (u0 + c - RING + 1))
                eng.wait_ge(raw_in[slot], i * 16 + 16 * ((u0 + c) // RAW + 1))
                eng.activation(wh[:, slot, :], raw[:, slot, :], ACT.Copy).then_inc(w_hi, 1)

            with eng.Fori(0, KH // 2) as i:
                for q in range(2):
                    pair = i * 2 + q
                    done = first_tap + 6 * q
                    unit_hi(i, 2 * q + LEAD)
                    for v, (buf, signal) in enumerate(((gpad, g_in), (vpad, v_in))):
                        eng.wait_ge(w_used, i * 4 + (u0 + 2 * q + v + 1))
                        eng.wait_ge(tap, i * 12 + (done - 3 + 3 * v))
                        c = pair * 2 + (C_FUP_B + 2 * KH * layer + v)
                        eng.activation(buf[:, FPAD:], ps[:, bank0 + 2 * q + v, :], ACT.Identity,
                                       bias=par[:, bass.ds(c, 1)]).then_inc(signal, 1)
                        if v == 0:
                            unit_hi(i, 2 * q + 1 + LEAD)
                    eng.wait_ge(tap, i * 12 + (done + 3))
                    eng.activation(gacc[:, :], gacc[:, :], ACT.Silu).then_inc(gs, 1)
                    eng.wait_ge(pr, i * 2 + (layer * KH + q + 1))
                    eng.activation(hh[:, bass.ds(pair, 1), :].rearrange("p o n -> p (o n)"), prod[:, :], ACT.Copy).then_inc(h_hi, 1)

        norm_hi(0, U_UP0)
        ffn_up(0, U_UP0, 4)
        his(range(U_DOWN0 + LEAD, U_GV))
        norm_hi(1, U_GV)

        his([U_GV + 3])
        for h in range(2):
            for t in range(NT):
                eng.wait_ge(v_ev, h * NT + t + 1)
                eng.activation(vtm[:, t, h * HALF:(h + 1) * HALF], vtm[:, t, h * HALF:(h + 1) * HALF], ACT.Gelu).then_inc(v_gelu, 1)
                if h == 0:
                    his([U_GV + 4 + t])
                else:
                    his([U_GU + t])
        eng.wait_ge(ws_m, 1)
        eng.activation(wsh[:, :, :], wsraw[:, :, :], ACT.Copy).then_inc(ws_hi, 1)
        for j in range(KD):
            eng.wait_ge(w_used, U_GU + j + 1)
            eng.activation(uu[:, j, :], ps[:, 4 + j % 4, :], ACT.Gelu, bias=par[:, C_GU_B + j:C_GU_B + j + 1]).then_inc(u_gelu, 1)
            his([U_GU + 4 + j])
            if j % 2 == 0:
                t = j // 2
                eng.wait_ge(v_n, t + 1)
                eng.activation(vh[:, t, :], vtm[:, t, :], ACT.Copy).then_inc(v_hi, 1)
        for g in range(GROUPS):
            eng.wait_ge(us_s, g + 1)
            if g == 0:
                eng.wait_ge(v_lo, NT)
            eng.activation(ush[:, g, :], uu[:, g, :], ACT.Copy).then_inc(us_hi, 1)
            if g % 2 and g >= 3:
                his([U_GOUT + 4 + (g - 3) // 2])
        his([U_GOUT + 7])
        norm_hi(2, U_UP1)
        ffn_up(1, U_UP1, 0)
        his(range(U_DOWN1 + LEAD, UNITS))

    @block.vector
    def _(eng):
        def los(units):
            for u in units:
                if u >= UNITS:
                    return
                if u >= RING:
                    eng.wait_ge(w_used, u - RING + 1)
                eng.wait_ge(w_hi, u + 1)
                eng.tensor_tensor(wl[:, u % RING, :], raw[:, u % RAW, :], wh[:, u % RING, :].bitcast(f32), ALU.subtract).then_inc(w_lo, 1)

        def first_lo(c):
            eng.wait_ge(x_hi, c + 1)
            eng.tensor_tensor(xl[:, 2 * c:2 * c + 2, :], xraw[:, 2 * c:2 * c + 2, :], xh[:, 2 * c:2 * c + 2, :].bitcast(f32),
                              ALU.subtract).then_inc(x_lo, 1)

        eng.memset(glu[:, :, 0:PAD], 0.0).then_inc(dw_ok, 1)
        eng.memset(gluh[:, :, 0:PAD].bitcast(f32), 0.0)
        eng.memset(glul[:, :, 0:PAD].bitcast(f32), 0.0)
        first_lo(0)
        los([0])
        for c in range(1, XCH):
            first_lo(c)
        eng.wait_ge(par_in, 16)
        eng.tensor_copy(dwh[:, :], par[:, C_CDW_W:C_CDW_W + KD * TAPS]).then_inc(st_ok, 1)
        eng.wait_ge(st_ok, 1)
        eng.tensor_tensor(dwl[:, :], par[:, C_CDW_W:C_CDW_W + KD * TAPS], dwh[:, :].bitcast(f32), ALU.subtract).then_inc(dw_ok, 1)
        los([1, 2])

        seq = [1]

        def stat(ins):
            seq[0] += 1
            ins.then_inc(st_ok, 1)
            return seq[0]

        for j in range(KD):
            los([2 * j + LEAD])
            eng.wait_ge(gate_s, j + 1)
            eng.wait_ge(w_used, 2 * j + 2)
            eng.scalar_tensor_tensor(out=glu[:, j % 2, PAD:CW], in0=ps[:, (2 * j + 1) % 4, :], scalar=par[:, C_CIN_B + j:C_CIN_B + j + 1],
                                     in1=sig[:, :], op0=ALU.add, op1=ALU.mult).then_inc(glu_s, 1)
            los([2 * j + 1 + LEAD])
            eng.wait_ge(glu_hi, j + 1)
            eng.tensor_tensor(glul[:, j % 2, PAD:CW], glu[:, j % 2, PAD:CW], gluh[:, j % 2, PAD:CW].bitcast(f32),
                              ALU.subtract).then_inc(glu_lo, 1)
            for k in range(DV_TAPS):
                c = C_CDW_W + j * TAPS + k
                n = j * DV_TAPS + k
                if k == 0:
                    eng.tensor_scalar(acc[:, 0, :], glu[:, j % 2, 0:SEQ], par[:, c:c + 1],
                                      par[:, C_CDW_B + j:C_CDW_B + j + 1], ALU.mult, ALU.add).then_inc(dw_tap, 1)
                elif k == 1:
                    eng.tensor_scalar(acc[:, 1, :], glu[:, j % 2, 1:1 + SEQ], par[:, c:c + 1], None, ALU.mult).then_inc(dw_tap, 1)
                else:
                    eng.wait_ge(dw_tap, n - 1)
                    eng.scalar_tensor_tensor(out=acc[:, k % 2, :], in0=glu[:, j % 2, k:k + SEQ], scalar=par[:, c:c + 1],
                                             in1=acc[:, k % 2, :], op0=ALU.mult, op1=ALU.add).then_inc(dw_tap, 1)
            eng.wait_ge(dw_tap, (j + 1) * DV_TAPS)
            n = stat(eng.tensor_tensor(acc[:, 0, :], acc[:, 0, :], acc[:, 1, :], ALU.add))
            eng.wait_ge(st_ok, n)
            eng.wait_ge(dw_pe, j + 1)
            if j >= 2:
                eng.wait_ge(ct_pe, j - 1)
            eng.tensor_tensor(cbuf[:, j % 2, :], acc[:, 0, :], ps[:, 4 + j % 2, :], ALU.add).then_inc(conv_c, 1)
            if j == 6:
                eng.wait_ge(ct_ok, 4)
                for t in range(NT):
                    n = stat(eng.bn_stats(stats[:, t, 0, :], ctm[:, t, 0:HALF]))
        eng.wait_ge(ct_ok, KD)
        for t in range(NT):
            n = stat(eng.bn_stats(stats[:, t, 1, :], ctm[:, t, HALF:D]))
        eng.wait_ge(st_ok, n)
        for t in range(NT - 1):
            stat(eng.bn_aggr(mv[:, t, :], stats[:, t, :, :].rearrange("p a b -> p (a b)")))
        t = NT - 1
        eng.bn_aggr(mv[:, t, :], stats[:, t, :, :].rearrange("p a b -> p (a b)")).then_inc(var_ok, 1)
        eng.wait_ge(var_ok, 1)
        eng.wait_ge(rstd_ok, 1)
        for t in range(NT):
            eng.tensor_scalar(ctm[:, t, :], ctm[:, t, :], mv[:, t, 0:1], rstd[:, t:t + 1], ALU.subtract, ALU.mult).then_inc(zc, 1)
        ahead = {0: U_CONV_OUT + 3, 3: U_CONV_OUT + 4, 5: U_CONV_OUT + 5, 7: U_CONV_OUT + 6}
        for k in range(KD):
            eng.wait_ge(x_hi, X0 + k + 1)
            eng.tensor_tensor(xl[:, k, :], slb[:, k % 2, :], xh[:, k, :].bitcast(f32), ALU.subtract).then_inc(x_lo, 1)
            if k in ahead:
                los([ahead[k]])
        los([U_CONV_OUT + 7])

        def first_half(n, t, u_half):
            if t == 0:
                eng.wait_ge(w_used, u_half)
                eng.wait_ge(res_ok, (n + 1) * NT)
            r = res[:, t, 0:HALF]
            k = stat(eng.tensor_tensor(r, r, ps[:, B0[n] + t, :], ALU.add))
            eng.wait_ge(st_ok, k)
            stat(eng.bn_stats(stats[:, t, 0, :], r))

        def second_half(n, t, u_end):
            m = n * NT + t + 1 + (NT if n >= 2 else 0)
            if t < NT - 1:
                eng.wait_ge(blk, (n + (n >= 2)) * (NT - 1) + t + 1)
            else:
                eng.wait_ge(w_used, u_end)
            r = res[:, t, HALF:D]
            k = stat(eng.tensor_tensor(r, r, ps[:, B1[n] + t, :], ALU.add))
            eng.wait_ge(st_ok, k)
            k = stat(eng.bn_stats(stats[:, t, 1, :], r))
            eng.wait_ge(st_ok, k)
            eng.bn_aggr(mv[:, t, :], stats[:, t, :, :].rearrange("p a b -> p (a b)")).then_inc(var_ok, 1)
            eng.wait_ge(var_ok, m + 1)
            if t == 0:
                eng.wait_ge(norm_in, 32 * (n + 1))
            r = res[:, t, :]
            eng.scalar_tensor_tensor(out=r, in0=r, scalar=mv[:, t, 0:1], in1=grow[:, :],
                                     op0=ALU.subtract, op1=ALU.mult).then_inc(nrm, 1)
            eng.wait_ge(nrm, n * NT + t + 1)
            eng.wait_ge(rstd_ok, m + 1)
            eng.scalar_tensor_tensor(out=r, in0=r, scalar=rstd[:, t:t + 1], in1=brow_n[:, :],
                                     op0=ALU.mult, op1=ALU.add).then_inc(x_ok, 1)

        def block_lo(n, t):
            x_before = XC + n * 2 * NT
            for q in range(2):
                eng.wait_ge(x_hi, x_before + 2 * t + q + 1)
                eng.tensor_tensor(xl[:, 4 * q:4 * q + 4, t * P:(t + 1) * P],
                                  ps[:, B0[n] + 2 * (t % 2) + q, :].rearrange("p (k n) -> p k n", k=4),
                                  xh[:, 4 * q:4 * q + 4, t * P:(t + 1) * P].bitcast(f32), ALU.subtract).then_inc(x_lo, 1)

        def norm(n, u_end):
            second_half(n, 0, u_end)
            second_half(n, 1, u_end)
            if n < 3:
                block_lo(n, 0)
            second_half(n, 2, u_end)
            if n < 3:
                block_lo(n, 1)
            second_half(n, 3, u_end)
            if n < 3:
                block_lo(n, 2)
                los([u_end])
                block_lo(n, 3)
                los([u_end + 1, u_end + 2])

        def ffn_up(layer, u0):
            ring = u0 % RING
            eng.wait_ge(x_ok, (2 * layer + 1) * NT)
            eng.memset(gpad[:, 0:FPAD], 0.0).then_inc(tap, PAD_TAPS // 2)
            eng.memset(vpad[:, 0:FPAD], 0.0).then_inc(tap, PAD_TAPS // 2)
            first_tap = PAD_TAPS * (layer + 1) + 6 * KH * layer
            eng.wait_ge(tap, first_tap)

            def unit_lo(i, c):
                slot = (ring + c) % RING
                eng.wait_ge(w_hi, i * 4 + (u0 + c + 1))
                eng.tensor_tensor(wl[:, slot, :], raw[:, slot, :], wh[:, slot, :].bitcast(f32), ALU.subtract).then_inc(w_lo, 1)

            with eng.Fori(0, KH // 2) as i:
                for q in range(2):
                    pair = i * 2 + q
                    done = first_tap + 6 * q
                    unit_lo(i, 2 * q + LEAD)
                    for v, (buf, sums, signal) in enumerate(((gpad, gacc, g_in), (vpad, vacc, v_in))):
                        eng.wait_ge(signal, pair + (layer * KH + 1))
                        cb = pair * 2 + (C_FDW_B + 2 * KH * layer + v)
                        for k in range(FTAPS):
                            cw = pair * (2 * FTAPS) + (C_FDW_W + FTAPS * (2 * KH * layer + v) + FTAPS - 1 - k)
                            off = FPAD - k
                            if k == 0:
                                eng.tensor_scalar(sums[:, :], buf[:, off:off + SEQ], par[:, bass.ds(cw, 1)], par[:, bass.ds(cb, 1)],
                                                  ALU.mult, ALU.add).then_inc(tap, 1)
                            else:
                                eng.wait_ge(tap, i * 12 + (done + 3 * v + k))
                                eng.scalar_tensor_tensor(out=sums[:, :], in0=buf[:, off:off + SEQ], scalar=par[:, bass.ds(cw, 1)],
                                                         in1=sums[:, :], op0=ALU.mult, op1=ALU.add).then_inc(tap, 1)
                    eng.wait_ge(tap, i * 12 + (done + 6))
                    eng.wait_ge(gs, pair + (layer * KH + 1))
                    eng.tensor_tensor(prod[:, :], gacc[:, :], vacc[:, :], ALU.mult).then_inc(pr, 1)
                    unit_lo(i, 2 * q + 1 + LEAD)
                    eng.wait_ge(h_hi, pair + (layer * KH + 1))
                    eng.tensor_tensor(hl[:, bass.ds(pair, 1), :].rearrange("p o n -> p (o n)"), prod[:, :],
                                      hh[:, bass.ds(pair, 1), :].rearrange("p o n -> p (o n)").bitcast(f32), ALU.subtract).then_inc(h_lo, 1)

        def ffn_down(n, u0):
            los(range(u0 + LEAD, u0 + 11 + 4))
            for t in range(NT):
                first_half(n, t, u0 + 11)
                los([u0 + 15 + t])
            los(range(u0 + 19, u0 + 22))
            norm(n, u0 + 22)

        for t in range(NT):
            first_half(0, t, U_CONV_OUT + 4)
        norm(0, U_UP0)
        ffn_up(0, U_UP0)
        ffn_down(1, U_DOWN0)

        los([U_GV + 3])
        eng.wait_ge(gm_in, 16 * 5)
        for h in range(2):
            for t in range(NT):
                if h == 0 and t < NT - 1:
                    eng.wait_ge(blk, 2 * (NT - 1) + t + 1)
                else:
                    eng.wait_ge(w_used, U_GV + 4 * (h + 1))
                cols = slice(h * HALF, (h + 1) * HALF)
                eng.tensor_tensor(vtm[:, t, cols], ps[:, 4 - 4 * h + t, :], gvrow[:, cols], ALU.add).then_inc(v_ev, 1)
                if h == 0:
                    los([U_GV + 4 + t])
                else:
                    los([U_GU + t])
                if t >= 1:
                    eng.wait_ge(v_gelu, h * NT + t)
                    n = stat(eng.bn_stats(stats[:, t - 1, h, :], vtm[:, t - 1, cols]))
            eng.wait_ge(v_gelu, (h + 1) * NT)
            n = stat(eng.bn_stats(stats[:, NT - 1, h, :], vtm[:, NT - 1, cols]))
        eng.wait_ge(st_ok, n)
        for t in range(NT):
            eng.bn_aggr(mv[:, t, :], stats[:, t, :, :].rearrange("p a b -> p (a b)")).then_inc(var_ok, 1)
        for t in range(NT):
            m = 1 + 2 * NT + t
            eng.wait_ge(var_ok, m + 1)
            k = stat(eng.scalar_tensor_tensor(out=vtm[:, t, :], in0=vtm[:, t, :], scalar=mv[:, t, 0:1], in1=glg[:, :],
                                              op0=ALU.subtract, op1=ALU.mult))
            eng.wait_ge(st_ok, k)
            eng.wait_ge(rstd_ok, m + 1)
            eng.scalar_tensor_tensor(out=vtm[:, t, :], in0=vtm[:, t, :], scalar=rstd[:, t:t + 1], in1=glb[:, :],
                                     op0=ALU.mult, op1=ALU.add).then_inc(v_n, 1)
            los([U_GU + 4 + 2 * t])
            eng.wait_ge(v_hi, t + 1)
            eng.tensor_tensor(vl[:, t, :], vtm[:, t, :], vh[:, t, :].bitcast(f32), ALU.subtract).then_inc(v_lo, 1)
            los([U_GU + 5 + 2 * t])
            if t == 0:
                eng.wait_ge(ws_hi, 1)
                eng.tensor_tensor(wsl[:, :, :], wsraw[:, :, :], wsh[:, :, :].bitcast(f32), ALU.subtract).then_inc(ws_lo, 1)
        for g in range(GROUPS):
            eng.wait_ge(sp, g + 1)
            bias = bsrow[:, g:g + 1, :].broadcast_to([P, NT, P])
            eng.tensor_tensor(ps[:, g % 4, :].rearrange("p (n t) -> p n t", n=NT), ps[:, g % 4, :].rearrange("p (n t) -> p n t", n=NT),
                              bias, ALU.add).then_inc(sp_b, 1)
            eng.wait_ge(sp_b, g + 1)
            eng.wait_ge(u_gelu, g + 1)
            eng.tensor_tensor(uu[:, g, :], ps[:, g % 4, :], uu[:, g, :], ALU.mult).then_inc(us_s, 1)
            if g % 2 and g >= 3:
                los([U_GOUT + 4 + (g - 3) // 2])
            eng.wait_ge(us_hi, g + 1)
            eng.tensor_tensor(usl[:, g, :], uu[:, g, :], ush[:, g, :].bitcast(f32), ALU.subtract).then_inc(us_lo, 1)
        los([U_GOUT + 7])
        for t in range(NT):
            first_half(2, t, U_GOUT + 4)
        norm(2, U_UP1)
        ffn_up(1, U_UP1)
        ffn_down(3, U_DOWN1)

    @block.tensor
    def _(eng):
        def up(slot, bank, mov_h, mov_l, before=None):
            for k in range(KD):
                if before is not None:
                    before(k)
                a, b = wh[:, slot, k * P:(k + 1) * P], wl[:, slot, k * P:(k + 1) * P]
                eng.matmul(ps[:, bank, :], a, mov_h[:, k, :], start=(k == 0), stop=False)
                eng.matmul(ps[:, bank, :], a, mov_l[:, k, :], start=False, stop=False)
                mm = eng.matmul(ps[:, bank, :], b, mov_h[:, k, :], start=False, stop=(k == KD - 1))
            return mm

        def down(u, c, t, bank, st_h, st_l, k, first, last):
            slot = u % RING
            w_h, w_l = wh[:, slot, c * HALF:(c + 1) * HALF], wl[:, slot, c * HALF:(c + 1) * HALF]
            s_h, s_l = st_h[:, k, t * P:(t + 1) * P], st_l[:, k, t * P:(t + 1) * P]
            eng.matmul(ps[:, bank + t, :], s_h, w_h, start=first, stop=False)
            eng.matmul(ps[:, bank + t, :], s_h, w_l, start=False, stop=False)
            return eng.matmul(ps[:, bank + t, :], s_l, w_h, start=False, stop=last)

        def down_by_k(u0, n, bank, st_h, st_l, k0, kn, before=None):
            for i in range(n):
                eng.wait_ge(w_lo, u0 + i + 1)
                for c in range(2):
                    k = k0 + 2 * i + c
                    if before is not None:
                        before(k)
                    for t in range(NT):
                        mm = down(u0 + i, c, t, bank, st_h, st_l, k, k == 0, k == kn - 1)
                mm.then_inc(w_used, 1)

        def down_by_block(u0, n, bank, st_h, st_l, k0, kn, before=None):
            for t in range(NT):
                if before is not None:
                    before(t)
                for i in range(n):
                    if t == 0:
                        eng.wait_ge(w_lo, u0 + i + 1)
                    for c in range(2):
                        k = k0 + 2 * i + c
                        mm = down(u0 + i, c, t, bank, st_h, st_l, k, k == 0, k == kn - 1)
                    if t == NT - 1:
                        mm.then_inc(w_used, 1)
                if t < NT - 1:
                    mm.then_inc(blk, 1)

        eng.wait_ge(const_ok, 3)

        def unit_conv(u):
            j = u // 2
            eng.wait_ge(w_lo, u + 1)
            if j >= 2:
                eng.wait_ge(glu_s if u % 2 else gate_s, j - 1)
            def before(k):
                if u == 0 and k % 2 == 0:
                    eng.wait_ge(x_lo, k // 2 + 1)
            up(u % RING, u % 4, xh, xl, before).then_inc(w_used, 1)

        def taps(j):
            eng.wait_ge(glu_lo, j + 1)
            eng.wait_ge(diag, 2 * (j + 1))
            if j >= 2:
                eng.wait_ge(conv_c, j - 1)
            b = j % 2
            for q in range(PE_TAPS):
                k = DV_TAPS + q
                eng.matmul(ps[:, 4 + b, :], diagh[:, b, q, :], gluh[:, b, k:k + SEQ], start=(q == 0), stop=False)
                eng.matmul(ps[:, 4 + b, :], diagh[:, b, q, :], glul[:, b, k:k + SEQ], start=False, stop=False)
                mm = eng.matmul(ps[:, 4 + b, :], diagl[:, b, q, :], gluh[:, b, k:k + SEQ], start=False, stop=(q == PE_TAPS - 1))
            mm.then_inc(dw_pe, 1)

        def to_tm(j):
            eng.wait_ge(conv_c, j + 1)
            if j >= 2:
                eng.wait_ge(ct_ok, j - 1)
            for t in range(NT):
                mm = eng.transpose(ps[:, 6 + j % 2, t * P:(t + 1) * P], cbuf[:, j % 2, t * P:(t + 1) * P], ident[:, :])
            mm.then_inc(ct_pe, 1)

        for j in range(KD + 2):
            if j < KD:
                unit_conv(2 * j)
                unit_conv(2 * j + 1)
            if 1 <= j <= KD:
                taps(j - 1)
            if j >= 2:
                to_tm(j - 2)

        def to_fm(k):
            if k == 0:
                eng.wait_ge(zc, NT)
            if k >= 2:
                eng.wait_ge(sl, k - 1)
            for t in range(NT):
                mm = eng.transpose(ps[:, 4 + k % 2, t * P:(t + 1) * P], ctm[:, t, k * P:(k + 1) * P], ident[:, :])
            mm.then_inc(zt, 1)

        def conv_tile(k):
            if k == 0:
                to_fm(0)
            if k == 0:
                to_fm(1)
            elif k + 1 < KD:
                to_fm(k + 1)
            eng.wait_ge(x_lo, X0 + k + 1)

        down_by_k(U_CONV_OUT, 4, 0, xh, xl, 0, KD, conv_tile)
        down_by_block(U_CONV_OUT + 4, 4, 4, xh, xl, 0, KD)

        def norm_fm(n):
            for t in range(NT):
                eng.wait_ge(x_ok, n * NT + t + 1)
                for q in range(2):
                    if t >= 2:
                        eng.wait_ge(x_lo, XC + n * 2 * NT + 2 * (t - 2) + q + 1)
                    for k in range(4):
                        mm = eng.transpose(ps[:, B0[n] + 2 * (t % 2) + q, k * P:(k + 1) * P],
                                           res[:, t, (4 * q + k) * P:(4 * q + k + 1) * P], ident[:, :])
                    mm.then_inc(xt, 1)

        def ffn(layer, n, u_up, u_down):
            eng.wait_ge(x_lo, XN[n - 1])
            ring = u_up % RING
            with eng.Fori(0, KH // 2) as i:
                for c in range(4):
                    eng.wait_ge(w_lo, i * 4 + (u_up + c + 1))
                    eng.wait_ge(tap, i * 12 + (PAD_TAPS * layer + 6 * KH * layer + 3 * c + 1))
                    up((ring + c) % RING, B1[n - 1] + c, xh, xl).then_inc(w_used, 1)
            seen = layer * KH

            def hidden(k):
                eng.wait_ge(h_lo, seen + k + 1)
            down_by_k(u_down, 11, B0[n], hh, hl, 0, KH, hidden)
            down_by_k(u_down + 11, 7, B1[n], hh, hl, 0, KH)
            down_by_block(u_down + 18, 4, B1[n], hh, hl, 14, KH)

        norm_fm(0)
        ffn(0, 1, U_UP0, U_DOWN0)
        norm_fm(1)

        down_by_block(U_GV, 4, 4, xh, xl, 0, KD, lambda t: eng.wait_ge(x_lo, XC + 2 * NT + 2 * (t + 1)))
        down_by_k(U_GV + 4, 4, 0, xh, xl, 0, KD)
        for j in range(KD):
            eng.wait_ge(w_lo, U_GU + j + 1)
            if j < 4:
                eng.wait_ge(v_ev, j + 1)
            else:
                eng.wait_ge(u_gelu, j - 3)
            up((U_GU + j) % RING, 4 + j % 4, xh, xl).then_inc(w_used, 1)

        def spatial(g):
            if g == 0:
                eng.wait_ge(ws_lo, 1)
                eng.wait_ge(v_lo, NT)
            if g >= 4:
                eng.wait_ge(us_s, g - 3)
            for n in range(NT):
                o = ps[:, g % 4, n * P:(n + 1) * P]
                a, b = vh[:, n, g * P:(g + 1) * P], vl[:, n, g * P:(g + 1) * P]
                eng.matmul(o, a, wsh[:, g, :], start=True, stop=False)
                eng.matmul(o, a, wsl[:, g, :], start=False, stop=False)
                mm = eng.matmul(o, b, wsh[:, g, :], start=False, stop=True)
            mm.then_inc(sp, 1)

        def gated(k):
            if k == 0:
                for g in range(4):
                    spatial(g)
                eng.wait_ge(u_gelu, KD)
            eng.wait_ge(us_lo, k + 1)
            if k + 4 < GROUPS:
                spatial(k + 4)

        down_by_k(U_GOUT, 4, 4, ush, usl, 0, KD, gated)
        down_by_block(U_GOUT + 4, 4, 0, ush, usl, 0, KD)
        norm_fm(2)
        ffn(1, 3, U_UP1, U_DOWN1)

    block.__exit__(None, None, None)


def kernel(**inputs):
    import numpy as np
    import concourse.bacc as bacc
    from concourse.bass_utils import run_bass_kernel_spmd

    a = {k: np.asarray(v) for k, v in inputs.items()}

    def up_units(w):
        return w.reshape(KD, P, -1, P).transpose(2, 1, 0, 3).reshape(-1, P, UNIT)

    def down_units(w):
        return w.reshape(-1, 2, P, 2, HALF).transpose(3, 0, 2, 1, 4).reshape(-1, P, UNIT)

    def interleaved(first, second):
        return np.stack([up_units(first), up_units(second)], 1).reshape(-1, P, UNIT)

    cin, gin = a["conv_w_in"][0], a["gmlp_w_in"][0]
    units = [interleaved(cin[:, D:], cin[:, :D]), down_units(a["conv_w_out"][0])]
    for layer in range(DEPTH):
        w = a["ffn_w_up"][layer]
        if layer == 1:
            units += [down_units(gin[:, D:]), up_units(gin[:, :D]), down_units(a["gmlp_w_out"][0])]
        units += [interleaved(w[:, :HID], w[:, HID:]), down_units(a["ffn_w_down"][layer])]
    weights = np.ascontiguousarray(np.concatenate(units))

    def columns(v):
        return v.reshape(-1, P).T

    def pairs(v):
        v = v.reshape(DEPTH, -1, 2, KH, P)
        return v.transpose(4, 0, 3, 2, 1).reshape(P, -1)

    dw = a["conv_w_dw"][0].reshape(TAPS, KD, P).transpose(2, 1, 0).reshape(P, -1)
    params = np.ascontiguousarray(np.concatenate([
        columns(a["conv_b_in"][0]), dw, columns(a["conv_b_dw"][0]), columns(a["conv_ln_g"][0]),
        columns(a["conv_ln_b"][0]), columns(a["gmlp_b_in"][0][:D]), pairs(a["ffn_b_up"]),
        pairs(a["ffn_w_dw"]), pairs(a["ffn_b_dw"])], 1))
    n1g, n1b, n2g, n2b = a["norm1_g"], a["norm1_b"], a["norm2_g"], a["norm2_b"]
    rows = np.ascontiguousarray(np.stack([
        n1g[0], n1b[0], n2g[0], n2b[0], n1g[1], n1b[1], n2g[1], n2b[1],
        a["conv_b_out"][0], a["ffn_b_down"][0], a["gmlp_b_out"][0], a["ffn_b_down"][1],
        a["gmlp_b_in"][0][D:], a["gmlp_ln_g"][0], a["gmlp_ln_b"][0], a["gmlp_b_s"][0].reshape(-1)]))
    x = a["x"].reshape(SEQ, D)
    arrays = {
        "d_x_tm": np.ascontiguousarray(x),
        "d_x_fm": np.ascontiguousarray(x.reshape(SEQ, KD, P).transpose(2, 1, 0)),
        "d_weights": weights,
        "d_params": params,
        "d_rows": rows,
        "d_spatial": np.ascontiguousarray(a["gmlp_w_s"][0].transpose(2, 0, 1)),
    }
    nc = bacc.Bacc("TRN2", target_bir_lowering=False, num_devices=1)
    args = [nc.dram_tensor(k, v.shape, mybir.dt.from_np(v.dtype), kind="ExternalInput").ap() for k, v in arrays.items()]
    out = nc.dram_tensor("d_out", (SEQ, D), mybir.dt.float32, kind="ExternalOutput").ap()
    build_trunk(nc, *args, out)
    r = run_bass_kernel_spmd(nc, [arrays], core_ids=[0])
    return r.results[0]["d_out"].reshape(1, SEQ, D)
```

```python
import concourse.bass as bass
from concourse import mybir

P = 128
D = 1024
SEQ = 512
DEPTH = 2
NT = SEQ // P
KD = D // P
HID = 2816
KH = HID // P
HALF = 512
TAPS = 31
PAD = TAPS - 1
FTAPS = 3
FPAD = FTAPS - 1
GROUPS = 8
ALPHA = (2.0 * DEPTH) ** 0.25
EPS = 1e-5
UNIT = 1024

U_CONV_IN = 0
U_CONV_OUT = U_CONV_IN + 2 * KD
U_UP0 = U_CONV_OUT + KD
U_DOWN0 = U_UP0 + 2 * KH
U_GV = U_DOWN0 + KH
U_GU = U_GV + KD
U_GOUT = U_GU + KD
U_UP1 = U_GOUT + KD
U_DOWN1 = U_UP1 + 2 * KH
UNITS = U_DOWN1 + KH

RAW = 4
RING = 4
LEAD = 3
LAST = 4

EARLY = (U_UP0, U_GV, U_UP1)
IS_EARLY = [any(e <= u < e + RING for e in EARLY) for u in range(UNITS)]
IN_RING = [u for u in range(UNITS) if not IS_EARLY[u]]

PE_TAPS = [11] * (KD - 1) + [16]
DV_TAPS = [TAPS - n for n in PE_TAPS]

C_CIN_B = 0
C_CDW_W = C_CIN_B + 2 * KD
C_CDW_B = C_CDW_W + KD * TAPS
C_CLN_G = C_CDW_B + KD
C_CLN_B = C_CLN_G + KD
C_GU_B = C_CLN_B + KD
C_FUP_B = C_GU_B + KD
C_FDW_W = C_FUP_B + DEPTH * KH * 2
C_FDW_B = C_FDW_W + DEPTH * KH * 2 * FTAPS
NPAR = C_FDW_B + DEPTH * KH * 2

(R_N1G, R_N1B, R_N2G, R_N2B, R_N3G, R_N3B, R_N4G, R_N4B, R_BO1, R_BO2, R_BO3, R_BO4,
 R_GVB, R_GLG, R_GLB, R_GBS, NROW) = range(17)


def build_trunk(nc, x_tm_d, x_fm_d, weights_d, params_d, rows_d, spatial_d, out_d):
    f32 = mybir.dt.float32
    f32r = mybir.dt.float32r
    ALU = mybir.AluOpType
    ACT = mybir.ActivationFunctionType

    base = (nc.sbuf_base + 63) // 64 * 64
    at = [base]

    def place(name, shape, dt, offset=None):
        size = 4
        for n in shape[1:]:
            size *= n
        if offset is None:
            offset = at[0]
            at[0] += (size + 31) // 32 * 32
        return nc.alloc_sbuf_tensor_at(name, shape, dt, offset=offset)

    raw = place("raw", [P, RAW, UNIT], f32)
    wh = place("wh", [P, RING, UNIT], f32r)
    wl = place("wl", [P, RING, UNIT], f32r)
    xh = place("xh", [P, KD, SEQ], f32r)
    xl = place("xl", [P, KD, SEQ], f32r)
    res = place("res", [P, NT, D], f32)
    par = place("par", [P, NPAR], f32)
    brow = place("brow", [P, D], f32)
    ident = place("ident", [P, P], f32)
    half_m = place("half_m", [P, NT], f32)
    stats = place("stats", [P, NT, 3, 6], f32)
    mv = place("mv", [P, NT, 2], f32)
    veps = place("veps", [P, NT], f32)
    rstd = place("rstd", [P, NT], f32)
    sums = place("sums", [P, NT, 2], f32)
    negm = place("negm", [P, NT], f32)
    sqs = place("sqs", [P, NT], f32)

    s0 = at[0]
    at[0] += 2 * 2080 + 4 * 2048
    grow = place("grow", [P, D], f32, s0)
    brow_n = place("brow_n", [P, D], f32, s0 + 4096)
    bsrow = place("bsrow", [P, GROUPS, P], f32, s0 + 8192)
    gpad = place("gpad", [P, FPAD + SEQ], f32, s0)
    vpad = place("vpad", [P, FPAD + SEQ], f32, s0 + 2080)
    gacc = place("gacc", [P, SEQ], f32, s0 + 4160)
    vacc = place("vacc", [P, SEQ], f32, s0 + 4160 + 2048)
    prod = place("prod", [P, SEQ], f32, s0 + 4160 + 4096)

    h0 = at[0]
    hh = place("hh", [P, KH, SEQ], f32r)
    hl = place("hl", [P, KH, SEQ], f32r)
    assert at[0] <= nc.sbuf_usable_end, (at[0], nc.sbuf_usable_end)
    hend = at[0]
    at[0] = h0
    CW = PAD + SEQ
    xraw = place("xraw", [P, KD, SEQ], f32)
    glu = place("glu", [P, 2, CW], f32)
    gluh = place("gluh", [P, 2, CW], f32r)
    glul = place("glul", [P, 2, CW], f32r)
    sig = place("sig", [P, SEQ], f32)
    acc = place("acc", [P, 2, SEQ], f32)
    cbuf = place("cbuf", [P, 2, SEQ], f32)
    dwl = place("dwl", [P, KD * TAPS], f32)
    dwh = place("dwh", [P, KD * TAPS], f32r)
    diagh = [place(f"diagh{b}", [P, PE_TAPS[KD - 2 + b], P], f32r) for b in range(2)]
    diagl = [place(f"diagl{b}", [P, PE_TAPS[KD - 2 + b], P], f32r) for b in range(2)]
    ctm = place("ctm", [P, NT, D], f32)
    slb = place("slb", [P, 2, SEQ], f32)
    assert at[0] <= hend
    eh = place("eh", [P, RING, UNIT], f32r, h0 + 4096)
    el = place("el", [P, RING, UNIT], f32r, h0 + 49152)
    scaled = place("scaled", [P, D], f32, h0)
    squares = place("squares", [P, D], f32, h0 + 20480)
    wsraw = place("wsraw", [P, GROUPS, P], f32, h0)
    vh = place("vh", [P, NT, D], f32r, h0 + 4096)
    uu = place("uu", [P, KD, SEQ], f32, h0 + 20480)
    gvrow = place("gvrow", [P, D], f32, h0 + 36864)
    glg = place("glg", [P, D], f32, h0 + 36864 + 4096)
    glb = place("glb", [P, D], f32, h0 + 36864 + 8192)
    vl = place("vl", [P, NT, D], f32r, h0 + 49152)
    vtm = place("vtm", [P, NT, D], f32, h0 + 65536)
    wsh = place("wsh", [P, GROUPS, P], f32r, h0 + 81920)
    wsl = place("wsl", [P, GROUPS, P], f32r, h0 + 81920 + 4096)

    ps = nc.alloc_psum_tensor("ps", [P, 8, 512], f32)

    sem = nc.alloc_semaphore
    raw_in = [sem(f"raw_in{i}") for i in range(RAW)]
    xfm_in = [sem(f"xfm_in{i}") for i in range(KD)]
    xtm_in = sem("xtm_in")
    par_in = sem("par_in")
    bo_in = sem("bo_in")
    norm_in = sem("norm_in")
    gv_in = sem("gv_in")
    gm_in = sem("gm_in")
    out_done = sem("out_done")
    const_ok = sem("const_ok")
    w_hi = sem("w_hi")
    w_lo = sem("w_lo")
    w_used = sem("w_used")
    x_hi = sem("x_hi")
    x_lo = sem("x_lo")
    res0_ok = sem("res0_ok")
    res_ok = sem("res_ok")
    res_mul = sem("res_mul")
    dw_ok = sem("dw_ok")
    diag = sem("diag")
    gate_s = sem("gate_s")
    glu_s = sem("glu_s")
    glu_hi = sem("glu_hi")
    glu_lo = sem("glu_lo")
    dw_pe = sem("dw_pe")
    dw_tap = sem("dw_tap")
    conv_c = sem("conv_c")
    ct_pe = sem("ct_pe")
    ct_ok = sem("ct_ok")
    zc = sem("zc")
    zt = sem("zt")
    sl = sem("sl")
    blk = sem("blk")
    st_ok = sem("st_ok")
    var_ok = sem("var_ok")
    mean_ok = sem("mean_ok")
    sq_ok = sem("sq_ok")
    eps_ok = sem("eps_ok")
    rstd_ok = sem("rstd_ok")
    nrm = sem("nrm")
    x_ok = sem("x_ok")
    xt = sem("xt")
    g_in = sem("g_in")
    v_in = sem("v_in")
    tap = sem("tap")
    PAD_TAPS = 2 * 2 * FTAPS
    gs = sem("gs")
    pr = sem("pr")
    h_hi = sem("h_hi")
    h_lo = sem("h_lo")
    v_ev = sem("v_ev")
    v_gelu = sem("v_gelu")
    u_gelu = sem("u_gelu")
    v_n = sem("v_n")
    v_hi = sem("v_hi")
    v_lo = sem("v_lo")
    ws_m = sem("ws_m")
    ws_hi = sem("ws_hi")
    ws_lo = sem("ws_lo")
    sp = sem("sp")
    sp_b = sem("sp_b")
    us_s = sem("us_s")
    us_hi = sem("us_hi")
    us_lo = sem("us_lo")

    blk_of = [0, NT - 1, 3 * (NT - 1), 4 * (NT - 1)]
    X0 = KD
    XC = X0 + KD
    XN = [XC + 2 * NT * (n + 1) for n in range(3)]
    B0 = [0, 0, 4, 4]
    B1 = [4, 4, 0, 0]

    def split_at(u):
        if IS_EARLY[u]:
            q = (u - max(e for e in EARLY if e <= u)) % RING
            return eh[:, q, :], el[:, q, :]
        q = IN_RING.index(u) % RING
        return wh[:, q, :], wl[:, q, :]

    def wait_split(eng, u):
        if u == U_UP0:
            eng.wait_ge(w_used, U_CONV_OUT + 4)
        elif u == U_GV:
            eng.wait_ge(w_used, U_GV - LAST)
        elif u == U_UP1:
            eng.wait_ge(sp, GROUPS)
        elif not IS_EARLY[u] and IN_RING.index(u) >= RING:
            eng.wait_ge(w_used, IN_RING[IN_RING.index(u) - RING] + 1)

    block = nc.Block()
    block.__enter__()

    @block.sync
    def _(eng):
        def load(slot, unit):
            eng.dma_start(raw[:, slot, :], weights_d[bass.ds(unit, 1), :, :].rearrange("o p n -> p (o n)")
                          ).then_inc(raw_in[slot], 16)

        load(0, 0)
        load(1, 1)
        eng.dma_start(par[:, :], params_d).then_inc(par_in, 16)
        load(2, 2)
        load(3, 3)
        eng.wait_ge(x_lo, KD)
        eng.dma_start(brow[:, :], rows_d[R_BO1:R_BO1 + 1, :].partition_broadcast(P)).then_inc(bo_in, 16)
        for t in range(NT):
            eng.dma_start(res[:, t, :], x_tm_d[t * P:(t + 1) * P, :]).then_inc(xtm_in, 16)
        eng.dma_start(grow[:, :], rows_d[R_N1G:R_N1G + 1, :].partition_broadcast(P)).then_inc(norm_in, 16)
        eng.dma_start(brow_n[:, :], rows_d[R_N1B:R_N1B + 1, :].partition_broadcast(P)).then_inc(norm_in, 16)
        with eng.Fori(1, UNITS // RAW) as i:
            for s in range(RAW):
                eng.wait_ge(w_lo, i * RAW + (s - RAW + 1))
                load(s, i * RAW + s)
        for t in range(NT):
            eng.wait_ge(x_ok, 3 * NT + t + 1)
            eng.dma_start(out_d[t * P:(t + 1) * P, :], res[:, t, :]).then_inc(out_done, 16)
        eng.wait_ge(out_done, 16 * NT)

    @block.gpsimd
    def _(eng):
        def root(k, t, n):
            eng.wait_ge(eps_ok, k + 1)
            eng.tensor_tensor(rstd[:, t:t + n], veps[:, t:t + n], half_m[:, t:t + n], ALU.pow).then_inc(rstd_ok, 1)

        def mixer_root(k, seen, t, n):
            eng.wait_ge(var_ok, seen)
            eng.tensor_scalar(veps[:, t:t + n], mv[:, t:t + n, 1], EPS, None, ALU.add).then_inc(eps_ok, 1)
            root(k, t, n)

        def norm_root(k, seen, t):
            eng.wait_ge(sq_ok, seen)
            eng.tensor_scalar(veps[:, t:t + 1], sqs[:, t:t + 1], 1.0 / D, EPS, ALU.mult, ALU.add).then_inc(eps_ok, 1)
            root(k, t, 1)

        eng.memset(half_m[:, :], -0.5).then_inc(const_ok, 1)
        eng.memset(ident[:, :], 0.0).then_inc(const_ok, 1)
        eng.wait_ge(const_ok, 2)
        eng.affine_select(out=ident[:, :], in_=ident[:, :], compare_op=ALU.not_equal, fill=1.0, base=0,
                          pattern=[[-1, P]], channel_multiplier=1).then_inc(const_ok, 1)
        eng.wait_ge(xtm_in, 16 * NT)
        eng.wait_ge(bo_in, 16)
        for t in range(NT):
            eng.tensor_scalar(res[:, t, :], res[:, t, :], ALPHA, None, ALU.mult).then_inc(res_mul, 1)
            eng.wait_ge(res_mul, t + 1)
            eng.tensor_tensor(res[:, t, :], res[:, t, :], brow[:, :], ALU.add).then_inc(res0_ok, 1)

        mixer_root(0, 1, 0, NT)
        for n in range(2):
            for t in range(NT):
                norm_root(1 + n * NT + t, n * NT + t + 1, t)
        eng.wait_ge(gm_in, 16 * 4)
        eng.affine_select(out=wsraw[:, :, :], in_=wsraw[:, :, :], compare_op=ALU.is_ge, fill=0.0,
                          base=0, pattern=[[0, GROUPS], [1, P]], channel_multiplier=-1).then_inc(ws_m, 1)
        for t in range(NT):
            mixer_root(1 + 2 * NT + t, t + 2, t, 1)
        for n in range(2, 4):
            for t in range(NT):
                norm_root(1 + (n + 1) * NT + t, n * NT + t + 1, t)

    @block.scalar
    def _(eng):
        def his(units):
            for u in units:
                if u < UNITS:
                    wait_split(eng, u)
                    eng.wait_ge(raw_in[u % RAW], 16 + u // RAW * 16)
                    eng.activation(split_at(u)[0], raw[:, u % RAW, :], ACT.Copy).then_inc(w_hi, 1)

        def row(dst, r, s):
            eng.dma_start(dst, rows_d[r:r + 1, :].partition_broadcast(P)).then_inc(s, 16)

        def norm_rows(n):
            row(grow[:, :], R_N1G + 2 * n, norm_in)
            row(brow_n[:, :], R_N1B + 2 * n, norm_in)

        for k in range(KD):
            eng.dma_start(xraw[:, k, :], x_fm_d[:, k, :]).then_inc(xfm_in[k], 16)
        for k in range(KD):
            eng.wait_ge(xfm_in[k], 16)
            eng.activation(xh[:, k, :], xraw[:, k, :], ACT.Copy).then_inc(x_hi, 1)
            if k == 0:
                his([0])
        his(range(1, LEAD))
        eng.wait_ge(par_in, 16)
        eng.wait_ge(const_ok, 3)

        def diagonals(j):
            if j == 0:
                eng.wait_ge(dw_ok, 2)
            if j >= 2:
                eng.wait_ge(dw_pe, j - 1)
            for q in range(PE_TAPS[j]):
                c = j * TAPS + DV_TAPS[j] + q
                eng.activation(diagh[j % 2][:, q, :], ident[:, :], ACT.Copy, scale=par[:, C_CDW_W + c:C_CDW_W + c + 1])
                last = eng.activation(diagl[j % 2][:, q, :], ident[:, :], ACT.Copy, scale=dwl[:, c:c + 1])
            last.then_inc(diag, 1)

        def ct_out(j):
            eng.wait_ge(ct_pe, j + 1)
            eng.activation(ctm[:, :, j * P:(j + 1) * P],
                           ps[:, 6 + j % 2, :].rearrange("p (t n) -> p t n", t=NT), ACT.Copy).then_inc(ct_ok, 1)

        diagonals(0)
        for j in range(KD):
            his([2 * j + LEAD])
            eng.wait_ge(w_used, 2 * j + 1)
            if j >= 1:
                eng.wait_ge(glu_s, j)
            b = C_CIN_B + KD + j
            eng.activation(sig[:, :], ps[:, 2 * j % 4, :], ACT.Sigmoid, bias=par[:, b:b + 1]).then_inc(gate_s, 1)
            eng.wait_ge(glu_s, j + 1)
            if j >= 2:
                eng.wait_ge(dw_pe, j - 1)
            eng.activation(gluh[:, j % 2, PAD:CW], glu[:, j % 2, PAD:CW], ACT.Copy).then_inc(glu_hi, 1)
            his([2 * j + 1 + LEAD])
            if j >= 2:
                ct_out(j - 2)
            if j + 1 < KD:
                diagonals(j + 1)
        eng.wait_ge(res0_ok, NT)
        row(brow[:, :], R_BO2, bo_in)
        ct_out(KD - 2)
        ct_out(KD - 1)

        ahead = {0: U_CONV_OUT + 3, 3: U_CONV_OUT + 4, 5: U_CONV_OUT + 5, 7: U_CONV_OUT + 6}
        for k in range(KD):
            eng.wait_ge(zt, k + 1)
            if k >= 2:
                eng.wait_ge(x_lo, X0 + k - 1)
            eng.activation(slb[:, k % 2, :], ps[:, 4 + k % 2, :], ACT.Silu, scale=par[:, C_CLN_G + k:C_CLN_G + k + 1],
                           bias=par[:, C_CLN_B + k:C_CLN_B + k + 1]).then_inc(sl, 1)
            eng.wait_ge(sl, k + 1)
            eng.activation(xh[:, k, :], slb[:, k % 2, :], ACT.Copy).then_inc(x_hi, 1)
            if k in ahead:
                his([ahead[k]])
        his([U_CONV_OUT + 7])
        his(range(U_UP0, U_UP0 + RING))

        def squared(n, t):
            eng.wait_ge(mean_ok, n * NT + t + 1)
            eng.activation(squares[:, :], res[:, t, :], ACT.Square, bias=negm[:, t:t + 1],
                           accum_out=sqs[:, t:t + 1]).then_inc(sq_ok, 1)

        def block_hi(n, t):
            for q in range(2):
                eng.wait_ge(xt, 2 * (n * NT + t) + q + 1)
                eng.activation(xh[:, 4 * q:4 * q + 4, t * P:(t + 1) * P],
                               ps[:, B0[n] + 2 * (t % 2) + q, :].rearrange("p (k n) -> p k n", k=4), ACT.Copy).then_inc(x_hi, 1)

        def norm(n):
            for t in range(NT - 1):
                squared(n, t)
            if n < 3:
                for t in range(NT - 1):
                    block_hi(n, t)
            squared(n, NT - 1)
            if n < 3:
                block_hi(n, NT - 1)

        def ffn_up(layer, u0, bank0):
            first_tap = PAD_TAPS * (layer + 1) + 6 * KH * layer
            slot0 = IN_RING.index(u0 + RING) % RING

            def tile(i, q, ahead):
                pair = i * 2 + q
                done = first_tap + 6 * q
                ahead(2 * q)
                for v, (buf, signal) in enumerate(((gpad, g_in), (vpad, v_in))):
                    eng.wait_ge(w_used, i * 4 + (u0 + 2 * q + v + 1))
                    eng.wait_ge(tap, i * 12 + (done - 3 + 3 * v))
                    c = pair * 2 + (C_FUP_B + 2 * KH * layer + v)
                    eng.activation(buf[:, FPAD:], ps[:, bank0 + 2 * q + v, :], ACT.Identity,
                                   bias=par[:, bass.ds(c, 1)]).then_inc(signal, 1)
                    if v == 0:
                        ahead(2 * q + 1)
                eng.wait_ge(tap, i * 12 + (done + 3))
                eng.activation(gacc[:, :], gacc[:, :], ACT.Silu).then_inc(gs, 1)
                eng.wait_ge(pr, pair + (layer * KH + 1))
                eng.activation(hh[:, bass.ds(pair, 1), :].rearrange("p o n -> p (o n)"), prod[:, :], ACT.Copy).then_inc(h_hi, 1)

            for q in range(2):
                tile(0, q, lambda c: his([u0 + c + LEAD] if c else []))
            with eng.Fori(1, KH // 2) as i:
                def ahead(c):
                    slot, part = (slot0 + c + LEAD) % RING, (u0 + c + LEAD) % RAW
                    eng.wait_ge(w_used, i * 4 + (u0 + c + LEAD - RING + 1))
                    eng.wait_ge(raw_in[part], i * 16 + 16 * ((u0 + c + LEAD) // RAW + 1))
                    eng.activation(wh[:, slot, :], raw[:, part, :], ACT.Copy).then_inc(w_hi, 1)
                for q in range(2):
                    tile(i, q, ahead)

        norm(0)
        ffn_up(0, U_UP0, 4)
        eng.wait_ge(res_ok, NT)
        row(brow[:, :], R_BO3, bo_in)
        eng.wait_ge(h_lo, KH)
        norm_rows(1)
        his(range(U_DOWN0 + LEAD, U_GV + RING))
        norm(1)

        eng.wait_ge(w_used, U_GV)
        row(gvrow[:, :], R_GVB, gv_in)
        row(glg[:, :], R_GLG, gm_in)
        row(glb[:, :], R_GLB, gm_in)
        eng.wait_ge(x_ok, 2 * NT)
        eng.dma_start(wsraw[:, :, :], spatial_d).then_inc(gm_in, 16)
        row(bsrow[:, :, :].rearrange("p g t -> p (g t)"), R_GBS, gm_in)
        norm_rows(2)
        for h in range(2):
            for t in range(NT):
                eng.wait_ge(v_ev, h * NT + t + 1)
                eng.activation(vtm[:, t, h * HALF:(h + 1) * HALF], vtm[:, t, h * HALF:(h + 1) * HALF], ACT.Gelu).then_inc(v_gelu, 1)
                if h == 0:
                    his([U_GV + 4 + t])
            if h == 0:
                his(range(U_GU, U_GU + LEAD))
        his([U_GU + LEAD])
        eng.wait_ge(ws_m, 1)
        eng.activation(wsh[:, :, :], wsraw[:, :, :], ACT.Copy).then_inc(ws_hi, 1)
        for j in range(KD):
            eng.wait_ge(w_used, U_GU + j + 1)
            eng.activation(uu[:, j, :], ps[:, 4 + j % 4, :], ACT.Gelu, bias=par[:, C_GU_B + j:C_GU_B + j + 1]).then_inc(u_gelu, 1)
            his([U_GU + 4 + j])
            if j < NT:
                eng.wait_ge(v_n, j + 1)
                eng.activation(vh[:, j, :], vtm[:, j, :], ACT.Copy).then_inc(v_hi, 1)
        eng.wait_ge(res_ok, 2 * NT)
        row(brow[:, :], R_BO4, bo_in)
        for g in range(GROUPS):
            eng.wait_ge(us_s, g + 1)
            if g == 0:
                eng.wait_ge(w_used, U_GU + KD)
            eng.activation(xh[:, g, :], uu[:, g, :], ACT.Copy).then_inc(us_hi, 1)
            if g % 2 and g >= 3:
                his([U_GOUT + 4 + (g - 3) // 2])
        his([U_GOUT + 7])
        his(range(U_UP1, U_UP1 + RING))
        norm(2)
        ffn_up(1, U_UP1, 0)
        eng.wait_ge(h_lo, 2 * KH)
        norm_rows(3)
        his(range(U_DOWN1 + LEAD, UNITS))
        norm(3)

    @block.vector
    def _(eng):
        def los(units):
            for u in units:
                if u < UNITS:
                    wait_split(eng, u)
                    eng.wait_ge(w_hi, u + 1)
                    h, l = split_at(u)
                    eng.tensor_tensor(l, raw[:, u % RAW, :], h.bitcast(f32), ALU.subtract).then_inc(w_lo, 1)

        seq = [0]

        def stat(ins):
            seq[0] += 1
            ins.then_inc(st_ok, 1)
            return seq[0]

        eng.memset(glu[:, :, 0:PAD], 0.0).then_inc(dw_ok, 1)
        eng.memset(gluh[:, :, 0:PAD].bitcast(f32), 0.0)
        eng.memset(glul[:, :, 0:PAD].bitcast(f32), 0.0)
        for k in range(KD):
            eng.wait_ge(x_hi, k + 1)
            eng.tensor_tensor(xl[:, k, :], xraw[:, k, :], xh[:, k, :].bitcast(f32), ALU.subtract).then_inc(x_lo, 1)
            if k == 0:
                los([0])
        los([1])
        eng.wait_ge(par_in, 16)
        n = stat(eng.tensor_copy(dwh[:, :], par[:, C_CDW_W:C_CDW_W + KD * TAPS]))
        eng.wait_ge(st_ok, n)
        eng.tensor_tensor(dwl[:, :], par[:, C_CDW_W:C_CDW_W + KD * TAPS], dwh[:, :].bitcast(f32), ALU.subtract).then_inc(dw_ok, 1)
        los([2])

        taps_before = 0
        for j in range(KD):
            los([2 * j + LEAD])
            eng.wait_ge(gate_s, j + 1)
            eng.wait_ge(w_used, 2 * j + 2)
            eng.scalar_tensor_tensor(out=glu[:, j % 2, PAD:CW], in0=ps[:, (2 * j + 1) % 4, :], scalar=par[:, C_CIN_B + j:C_CIN_B + j + 1],
                                     in1=sig[:, :], op0=ALU.add, op1=ALU.mult).then_inc(glu_s, 1)
            los([2 * j + 1 + LEAD])
            eng.wait_ge(glu_hi, j + 1)
            eng.tensor_tensor(glul[:, j % 2, PAD:CW], glu[:, j % 2, PAD:CW], gluh[:, j % 2, PAD:CW].bitcast(f32),
                              ALU.subtract).then_inc(glu_lo, 1)
            for k in range(DV_TAPS[j]):
                c = C_CDW_W + j * TAPS + k
                if k == 0:
                    eng.tensor_scalar(acc[:, 0, :], glu[:, j % 2, 0:SEQ], par[:, c:c + 1],
                                      par[:, C_CDW_B + j:C_CDW_B + j + 1], ALU.mult, ALU.add).then_inc(dw_tap, 1)
                elif k == 1:
                    eng.tensor_scalar(acc[:, 1, :], glu[:, j % 2, 1:1 + SEQ], par[:, c:c + 1], None, ALU.mult).then_inc(dw_tap, 1)
                else:
                    eng.wait_ge(dw_tap, taps_before + k - 1)
                    eng.scalar_tensor_tensor(out=acc[:, k % 2, :], in0=glu[:, j % 2, k:k + SEQ], scalar=par[:, c:c + 1],
                                             in1=acc[:, k % 2, :], op0=ALU.mult, op1=ALU.add).then_inc(dw_tap, 1)
            taps_before += DV_TAPS[j]
            eng.wait_ge(dw_tap, taps_before)
            n = stat(eng.tensor_tensor(acc[:, 0, :], acc[:, 0, :], acc[:, 1, :], ALU.add))
            eng.wait_ge(st_ok, n)
            eng.wait_ge(dw_pe, j + 1)
            if j >= 2:
                eng.wait_ge(ct_pe, j - 1)
            eng.tensor_tensor(cbuf[:, j % 2, :], acc[:, 0, :], ps[:, 4 + j % 2, :], ALU.add).then_inc(conv_c, 1)
            if j == 6:
                eng.wait_ge(ct_ok, 4)
                for t in range(NT):
                    stat(eng.bn_stats(stats[:, t, 0, :], ctm[:, t, 0:HALF]))
        eng.wait_ge(ct_ok, KD - 1)
        for t in range(NT):
            stat(eng.bn_stats(stats[:, t, 1, :], ctm[:, t, HALF:D - P]))
        eng.wait_ge(ct_ok, KD)
        for t in range(NT):
            n = stat(eng.bn_stats(stats[:, t, 2, :], ctm[:, t, D - P:D]))
        eng.wait_ge(st_ok, n)
        for t in range(NT):
            ins = eng.bn_aggr(mv[:, t, :], stats[:, t, :, :].rearrange("p a b -> p (a b)"))
        ins.then_inc(var_ok, 1)
        eng.wait_ge(var_ok, 1)
        eng.wait_ge(rstd_ok, 1)
        for h in range(2):
            for t in range(NT):
                c = ctm[:, t, h * HALF:(h + 1) * HALF]
                eng.tensor_scalar(c, c, mv[:, t, 0:1], rstd[:, t:t + 1], ALU.subtract, ALU.mult).then_inc(zc, 1)
        ahead = {0: U_CONV_OUT + 3, 3: U_CONV_OUT + 4, 5: U_CONV_OUT + 5, 7: U_CONV_OUT + 6}
        for k in range(KD):
            eng.wait_ge(x_hi, X0 + k + 1)
            eng.tensor_tensor(xl[:, k, :], slb[:, k % 2, :], xh[:, k, :].bitcast(f32), ALU.subtract).then_inc(x_lo, 1)
            if k in ahead:
                los([ahead[k]])
        los([U_CONV_OUT + 7])

        def half_sum(n, t, h):
            r = res[:, t, h * HALF:(h + 1) * HALF]
            bank = (B1 if h else B0)[n] + t
            return stat(eng.scalar_tensor_tensor(out=r, in0=ps[:, bank, :], scalar=1.0, in1=r, op0=ALU.mult, op1=ALU.add,
                                                 accum_out=sums[:, t, h:h + 1]))

        def first_halves(n, u_half):
            eng.wait_ge(w_used, u_half)
            if n == 0:
                eng.wait_ge(res0_ok, NT)
            for t in range(NT):
                half_sum(n, t, 0)

        def second_half(n, t, u_end):
            if t < NT - 1:
                eng.wait_ge(blk, blk_of[n] + t + 1)
            else:
                eng.wait_ge(w_used, u_end)
            eng.wait_ge(st_ok, half_sum(n, t, 1))
            eng.tensor_scalar(negm[:, t:t + 1], sums[:, t, 0:1], sums[:, t, 1:2], -1.0 / D, ALU.add, ALU.mult).then_inc(mean_ok, 1)
            if t == 0:
                eng.wait_ge(norm_in, 32 * (n + 1))
            eng.wait_ge(mean_ok, n * NT + t + 1)
            eng.scalar_tensor_tensor(out=scaled[:, :], in0=res[:, t, :], scalar=negm[:, t:t + 1], in1=grow[:, :],
                                     op0=ALU.add, op1=ALU.mult).then_inc(nrm, 1)
            eng.wait_ge(nrm, n * NT + t + 1)
            eng.wait_ge(rstd_ok, 1 + n * NT + t + 1 + (NT if n >= 2 else 0))
            eng.scalar_tensor_tensor(out=res[:, t, :], in0=scaled[:, :], scalar=rstd[:, t:t + 1], in1=brow_n[:, :],
                                     op0=ALU.mult, op1=ALU.add).then_inc(x_ok, 1)

        def block_lo(n, t):
            for q in range(2):
                eng.wait_ge(x_hi, XC + n * 2 * NT + 2 * t + q + 1)
                eng.tensor_tensor(xl[:, 4 * q:4 * q + 4, t * P:(t + 1) * P],
                                  ps[:, B0[n] + 2 * (t % 2) + q, :].rearrange("p (k n) -> p k n", k=4),
                                  xh[:, 4 * q:4 * q + 4, t * P:(t + 1) * P].bitcast(f32), ALU.subtract).then_inc(x_lo, 1)

        def norm(n, u_end):
            for t in range(NT - 1):
                second_half(n, t, u_end)
            if n < 3:
                for t in range(NT - 1):
                    block_lo(n, t)
            second_half(n, NT - 1, u_end)
            if n < 3:
                block_lo(n, NT - 1)

        def residual(n):
            eng.wait_ge(bo_in, 16 * (n + 1))
            for t in range(NT):
                eng.scalar_tensor_tensor(out=res[:, t, :], in0=res[:, t, :], scalar=ALPHA, in1=brow[:, :],
                                         op0=ALU.mult, op1=ALU.add).then_inc(res_ok, 1)

        def ffn_up(layer, u0):
            slot0 = IN_RING.index(u0 + RING) % RING
            first_tap = PAD_TAPS * (layer + 1) + 6 * KH * layer
            eng.wait_ge(x_ok, (2 * layer + 1) * NT)
            eng.memset(gpad[:, 0:FPAD], 0.0).then_inc(tap, PAD_TAPS // 2)
            eng.memset(vpad[:, 0:FPAD], 0.0).then_inc(tap, PAD_TAPS // 2)
            eng.wait_ge(tap, first_tap)

            def tile(i, q, ahead):
                pair = i * 2 + q
                done = first_tap + 6 * q
                ahead(2 * q)
                for v, (buf, sums_v, signal) in enumerate(((gpad, gacc, g_in), (vpad, vacc, v_in))):
                    eng.wait_ge(signal, pair + (layer * KH + 1))
                    cb = pair * 2 + (C_FDW_B + 2 * KH * layer + v)
                    for k in range(FTAPS):
                        cw = pair * (2 * FTAPS) + (C_FDW_W + FTAPS * (2 * KH * layer + v) + FTAPS - 1 - k)
                        off = FPAD - k
                        if k == 0:
                            eng.tensor_scalar(sums_v[:, :], buf[:, off:off + SEQ], par[:, bass.ds(cw, 1)], par[:, bass.ds(cb, 1)],
                                              ALU.mult, ALU.add).then_inc(tap, 1)
                        else:
                            eng.wait_ge(tap, i * 12 + (done + 3 * v + k))
                            eng.scalar_tensor_tensor(out=sums_v[:, :], in0=buf[:, off:off + SEQ], scalar=par[:, bass.ds(cw, 1)],
                                                     in1=sums_v[:, :], op0=ALU.mult, op1=ALU.add).then_inc(tap, 1)
                eng.wait_ge(tap, i * 12 + (done + 6))
                eng.wait_ge(gs, pair + (layer * KH + 1))
                eng.tensor_tensor(prod[:, :], gacc[:, :], vacc[:, :], ALU.mult).then_inc(pr, 1)
                ahead(2 * q + 1)
                eng.wait_ge(h_hi, pair + (layer * KH + 1))
                eng.tensor_tensor(hl[:, bass.ds(pair, 1), :].rearrange("p o n -> p (o n)"), prod[:, :],
                                  hh[:, bass.ds(pair, 1), :].rearrange("p o n -> p (o n)").bitcast(f32), ALU.subtract).then_inc(h_lo, 1)

            for q in range(2):
                tile(0, q, lambda c: los([u0 + c + LEAD] if c else []))
            residual(2 * layer + 1)
            with eng.Fori(1, KH // 2) as i:
                def ahead(c):
                    slot, part = (slot0 + c + LEAD) % RING, (u0 + c + LEAD) % RAW
                    eng.wait_ge(w_hi, i * 4 + (u0 + c + LEAD + 1))
                    eng.tensor_tensor(wl[:, slot, :], raw[:, part, :], wh[:, slot, :].bitcast(f32), ALU.subtract).then_inc(w_lo, 1)
                for q in range(2):
                    tile(i, q, ahead)

        def ffn_down(n, u0):
            los(range(u0 + LEAD, u0 + KH // 2 + RING))
            first_halves(n, u0 + KH // 2)
            los(range(u0 + KH // 2 + RING, u0 + KH + (RING if n < 3 else 0)))
            norm(n, u0 + KH)

        first_halves(0, U_CONV_OUT + 4)
        los(range(U_UP0, U_UP0 + RING))
        norm(0, U_UP0)
        ffn_up(0, U_UP0)
        ffn_down(1, U_DOWN0)

        eng.wait_ge(gv_in, 16)
        for h in range(2):
            for t in range(NT):
                if h == 0 and t < NT - 1:
                    eng.wait_ge(blk, 2 * (NT - 1) + t + 1)
                else:
                    eng.wait_ge(w_used, U_GV + 4 * (h + 1))
                cols = slice(h * HALF, (h + 1) * HALF)
                eng.tensor_tensor(vtm[:, t, cols], ps[:, 4 - 4 * h + t, :], gvrow[:, cols], ALU.add).then_inc(v_ev, 1)
                if h == 0:
                    los([U_GV + 4 + t])
                if t >= 1:
                    eng.wait_ge(v_gelu, h * NT + t)
                    stat(eng.bn_stats(stats[:, t - 1, h, :], vtm[:, t - 1, cols]))
            eng.wait_ge(v_gelu, (h + 1) * NT)
            n = stat(eng.bn_stats(stats[:, NT - 1, h, :], vtm[:, NT - 1, cols]))
            if h == 0:
                los([U_GU])
                residual(2)
                los([U_GU + 1, U_GU + 2])
        los([U_GU + LEAD])
        eng.wait_ge(st_ok, n)
        for t in range(NT):
            eng.bn_aggr(mv[:, t, :], stats[:, t, 0:2, :].rearrange("p a b -> p (a b)")).then_inc(var_ok, 1)
        eng.wait_ge(gm_in, 16 * 4)
        for t in range(NT):
            eng.wait_ge(var_ok, t + 2)
            k = stat(eng.scalar_tensor_tensor(out=vtm[:, t, :], in0=vtm[:, t, :], scalar=mv[:, t, 0:1], in1=glg[:, :],
                                              op0=ALU.subtract, op1=ALU.mult))
            eng.wait_ge(st_ok, k)
            eng.wait_ge(rstd_ok, 1 + 2 * NT + t + 1)
            eng.scalar_tensor_tensor(out=vtm[:, t, :], in0=vtm[:, t, :], scalar=rstd[:, t:t + 1], in1=glb[:, :],
                                     op0=ALU.mult, op1=ALU.add).then_inc(v_n, 1)
            los([U_GU + 4 + t])
            eng.wait_ge(v_hi, t + 1)
            eng.tensor_tensor(vl[:, t, :], vtm[:, t, :], vh[:, t, :].bitcast(f32), ALU.subtract).then_inc(v_lo, 1)
            if t == 0:
                eng.wait_ge(ws_hi, 1)
                eng.tensor_tensor(wsl[:, :, :], wsraw[:, :, :], wsh[:, :, :].bitcast(f32), ALU.subtract).then_inc(ws_lo, 1)

        def gated(g):
            eng.wait_ge(sp, g + 1)
            bias = bsrow[:, g:g + 1, :].broadcast_to([P, NT, P])
            s_g = ps[:, g % 4, :].rearrange("p (n t) -> p n t", n=NT)
            eng.tensor_tensor(s_g, s_g, bias, ALU.add).then_inc(sp_b, 1)
            eng.wait_ge(sp_b, g + 1)
            eng.wait_ge(u_gelu, g + 1)
            eng.tensor_tensor(uu[:, g, :], ps[:, g % 4, :], uu[:, g, :], ALU.mult).then_inc(us_s, 1)

        los(range(U_GU + 8, U_GU + 10))
        gated(0)
        gated(1)
        los(range(U_GU + 10, U_GU + 12))
        for g in range(GROUPS):
            if g >= 2:
                gated(g)
            eng.wait_ge(us_hi, g + 1)
            eng.tensor_tensor(xl[:, g, :], uu[:, g, :], xh[:, g, :].bitcast(f32), ALU.subtract).then_inc(us_lo, 1)
            if g % 2 and g >= 3:
                los([U_GOUT + 4 + (g - 3) // 2])
        los([U_GOUT + 7])
        first_halves(2, U_GOUT + 4)
        los(range(U_UP1, U_UP1 + RING))
        norm(2, U_UP1)
        ffn_up(1, U_UP1)
        ffn_down(3, U_DOWN1)

    @block.tensor
    def _(eng):
        def up(w, bank, cols=slice(0, SEQ), before=None):
            w_h, w_l = w
            for k in range(KD):
                if before is not None:
                    before(k)
                a, b = w_h[:, k * P:(k + 1) * P], w_l[:, k * P:(k + 1) * P]
                eng.matmul(ps[:, bank, cols], a, xh[:, k, cols], start=(k == 0), stop=False)
                eng.matmul(ps[:, bank, cols], a, xl[:, k, cols], start=False, stop=False)
                mm = eng.matmul(ps[:, bank, cols], b, xh[:, k, cols], start=False, stop=(k == KD - 1))
            return mm

        def down(u, c, t, bank, st_h, st_l, k, first, last):
            h, l = split_at(u)
            w_h, w_l = h[:, c * HALF:(c + 1) * HALF], l[:, c * HALF:(c + 1) * HALF]
            s_h, s_l = st_h[:, k, t * P:(t + 1) * P], st_l[:, k, t * P:(t + 1) * P]
            eng.matmul(ps[:, bank + t, :], s_h, w_h, start=first, stop=False)
            eng.matmul(ps[:, bank + t, :], s_h, w_l, start=False, stop=False)
            return eng.matmul(ps[:, bank + t, :], s_l, w_h, start=False, stop=last)

        def down_by_k(u0, n, bank, st_h, st_l, k0, kn, before=None):
            for i in range(n):
                eng.wait_ge(w_lo, u0 + i + 1)
                for c in range(2):
                    k = k0 + 2 * i + c
                    if before is not None:
                        before(k)
                    for t in range(NT):
                        mm = down(u0 + i, c, t, bank, st_h, st_l, k, k == 0, k == kn - 1)
                mm.then_inc(w_used, 1)

        def down_by_block(u0, n, bank, st_h, st_l, k0, kn, after, before=None):
            for t in range(NT):
                if before is not None:
                    before(t)
                for i in range(n):
                    if t == 0:
                        eng.wait_ge(w_lo, u0 + i + 1)
                    for c in range(2):
                        k = k0 + 2 * i + c
                        mm = down(u0 + i, c, t, bank, st_h, st_l, k, k == 0, k == kn - 1)
                    if t == NT - 1:
                        mm.then_inc(w_used, 1)
                if t < NT - 1:
                    mm.then_inc(blk, 1)
                after(t)

        def unit_conv(u):
            j = u // 2
            eng.wait_ge(w_lo, u + 1)
            if j >= 2:
                eng.wait_ge(glu_s if u % 2 else gate_s, j - 1)

            def before(k):
                if u == 0:
                    eng.wait_ge(x_lo, k + 1)
            up(split_at(u), u % 4, before=before).then_inc(w_used, 1)

        def taps(j):
            eng.wait_ge(glu_lo, j + 1)
            eng.wait_ge(diag, j + 1)
            if j >= 2:
                eng.wait_ge(conv_c, j - 1)
            b, n = j % 2, PE_TAPS[j]
            for q in range(n):
                k = DV_TAPS[j] + q
                eng.matmul(ps[:, 4 + b, :], diagh[b][:, q, :], gluh[:, b, k:k + SEQ], start=(q == 0), stop=False)
                eng.matmul(ps[:, 4 + b, :], diagh[b][:, q, :], glul[:, b, k:k + SEQ], start=False, stop=False)
                mm = eng.matmul(ps[:, 4 + b, :], diagl[b][:, q, :], gluh[:, b, k:k + SEQ], start=False, stop=(q == n - 1))
            mm.then_inc(dw_pe, 1)

        def to_tm(j):
            eng.wait_ge(conv_c, j + 1)
            if j >= 2:
                eng.wait_ge(ct_ok, j - 1)
            for t in range(NT):
                mm = eng.transpose(ps[:, 6 + j % 2, t * P:(t + 1) * P], cbuf[:, j % 2, t * P:(t + 1) * P], ident[:, :])
            mm.then_inc(ct_pe, 1)

        for j in range(KD + 2):
            if j < KD:
                unit_conv(2 * j)
                unit_conv(2 * j + 1)
            if 1 <= j <= KD:
                taps(j - 1)
            if j >= 2:
                to_tm(j - 2)

        def to_fm(k):
            if k % 4 == 0:
                eng.wait_ge(zc, NT * (k // 4 + 1))
            if k >= 2:
                eng.wait_ge(sl, k - 1)
            for t in range(NT):
                mm = eng.transpose(ps[:, 4 + k % 2, t * P:(t + 1) * P], ctm[:, t, k * P:(k + 1) * P], ident[:, :])
            mm.then_inc(zt, 1)

        def conv_tile(k):
            if k == 0:
                to_fm(0)
                to_fm(1)
            elif k + 1 < KD:
                to_fm(k + 1)
            eng.wait_ge(x_lo, X0 + k + 1)

        def block_fm(n, t):
            eng.wait_ge(x_ok, n * NT + t + 1)
            for q in range(2):
                if t >= 2:
                    eng.wait_ge(x_lo, XC + n * 2 * NT + 2 * (t - 2) + q + 1)
                elif t == 0 and q == 0:
                    eng.wait_ge(mean_ok, n * NT + 1)
                for k in range(4):
                    mm = eng.transpose(ps[:, B0[n] + 2 * (t % 2) + q, k * P:(k + 1) * P],
                                       res[:, t, (4 * q + k) * P:(4 * q + k + 1) * P], ident[:, :])
                mm.then_inc(xt, 1)

        def after(n):
            def f(t):
                if t == 2 and n < 3:
                    block_fm(n, 0)
                    block_fm(n, 1)
                if t == 3 and n < 3:
                    block_fm(n, 2)
            return f

        def wait_x(n, t):
            eng.wait_ge(x_lo, XC + n * 2 * NT + 2 * (t + 1))

        down_by_k(U_CONV_OUT, 4, 0, xh, xl, 0, KD, conv_tile)
        down_by_block(U_CONV_OUT + 4, 4, 4, xh, xl, 0, KD, after(0))

        def ffn(layer, n, u_up, u_down):
            wait_x(n - 1, 2)
            early = (NT - 1) * P
            for c in range(2):
                eng.wait_ge(w_lo, u_up + c + 1)
                up(split_at(u_up + c), B1[n - 1] + c, slice(0, early))
            block_fm(n - 1, 3)
            wait_x(n - 1, 3)
            for c in range(4):
                eng.wait_ge(w_lo, u_up + c + 1)
                up(split_at(u_up + c), B1[n - 1] + c, slice(early if c < 2 else 0, SEQ)).then_inc(w_used, 1)
            slot0 = IN_RING.index(u_up + RING) % RING
            with eng.Fori(1, KH // 2) as i:
                for c in range(4):
                    eng.wait_ge(w_lo, i * 4 + (u_up + c + 1))
                    eng.wait_ge(tap, i * 12 + (PAD_TAPS * layer + 6 * KH * layer + 3 * c + 1))
                    slot = (slot0 + c) % RING
                    up((wh[:, slot, :], wl[:, slot, :]), B1[n - 1] + c).then_inc(w_used, 1)

            def hidden(k):
                eng.wait_ge(h_lo, layer * KH + k + 1)
            down_by_k(u_down, KH // 2, B0[n], hh, hl, 0, KH, hidden)
            down_by_k(u_down + KH // 2, KH // 2 - LAST, B1[n], hh, hl, 0, KH)
            down_by_block(u_down + KH - LAST, LAST, B1[n], hh, hl, KH - 2 * LAST, KH, after(n))

        ffn(0, 1, U_UP0, U_DOWN0)

        def last_block(t):
            if t == 1:
                block_fm(1, 3)
        down_by_block(U_GV, 4, 4, xh, xl, 0, KD, last_block, lambda t: wait_x(1, t))
        down_by_k(U_GV + 4, 4, 0, xh, xl, 0, KD)

        def spatial(g):
            if g == 0:
                eng.wait_ge(ws_lo, 1)
                eng.wait_ge(v_lo, NT)
            if g >= 4:
                eng.wait_ge(us_s, g - 3)
            for n in range(NT):
                o = ps[:, g % 4, n * P:(n + 1) * P]
                a, b = vh[:, n, g * P:(g + 1) * P], vl[:, n, g * P:(g + 1) * P]
                eng.matmul(o, a, wsh[:, g, :], start=True, stop=False)
                eng.matmul(o, a, wsl[:, g, :], start=False, stop=False)
                mm = eng.matmul(o, b, wsh[:, g, :], start=False, stop=True)
            mm.then_inc(sp, 1)

        for j in range(KD):
            eng.wait_ge(w_lo, U_GU + j + 1)
            if j < 4:
                eng.wait_ge(v_ev, j + 1)
            else:
                eng.wait_ge(u_gelu, j - 3)
            up(split_at(U_GU + j), 4 + j % 4).then_inc(w_used, 1)
            if j == KD - 2:
                for g in range(4):
                    spatial(g)

        def gated(k):
            if k == 0:
                eng.wait_ge(u_gelu, KD)
            eng.wait_ge(us_lo, k + 1)
            if k + 4 < GROUPS:
                spatial(k + 4)

        down_by_k(U_GOUT, 4, 4, xh, xl, 0, KD, gated)
        down_by_block(U_GOUT + 4, 4, 0, xh, xl, 0, KD, after(2))
        ffn(1, 3, U_UP1, U_DOWN1)

    block.__exit__(None, None, None)


def kernel(**inputs):
    import numpy as np
    import concourse.bacc as bacc
    from concourse.bass_utils import run_bass_kernel_spmd

    a = {k: np.asarray(v) for k, v in inputs.items()}

    def up_units(w):
        return w.reshape(KD, P, -1, P).transpose(2, 1, 0, 3).reshape(-1, P, UNIT)

    def down_units(w):
        return w.reshape(-1, 2, P, 2, HALF).transpose(3, 0, 2, 1, 4).reshape(-1, P, UNIT)

    def interleaved(first, second):
        return np.stack([up_units(first), up_units(second)], 1).reshape(-1, P, UNIT)

    cin, gin = a["conv_w_in"][0], a["gmlp_w_in"][0]
    units = [interleaved(cin[:, D:], cin[:, :D]), down_units(a["conv_w_out"][0])]
    for layer in range(DEPTH):
        w = a["ffn_w_up"][layer]
        if layer == 1:
            units += [down_units(gin[:, D:]), up_units(gin[:, :D]), down_units(a["gmlp_w_out"][0])]
        units += [interleaved(w[:, :HID], w[:, HID:]), down_units(a["ffn_w_down"][layer])]
    weights = np.ascontiguousarray(np.concatenate(units))

    def columns(v):
        return v.reshape(-1, P).T

    def pairs(v):
        v = v.reshape(DEPTH, -1, 2, KH, P)
        return v.transpose(4, 0, 3, 2, 1).reshape(P, -1)

    dw = a["conv_w_dw"][0].reshape(TAPS, KD, P).transpose(2, 1, 0).reshape(P, -1)
    params = np.ascontiguousarray(np.concatenate([
        columns(a["conv_b_in"][0]), dw, columns(a["conv_b_dw"][0]), columns(a["conv_ln_g"][0]),
        columns(a["conv_ln_b"][0]), columns(a["gmlp_b_in"][0][:D]), pairs(a["ffn_b_up"]),
        pairs(a["ffn_w_dw"]), pairs(a["ffn_b_dw"])], 1))
    n1g, n1b, n2g, n2b = a["norm1_g"], a["norm1_b"], a["norm2_g"], a["norm2_b"]
    rows = np.ascontiguousarray(np.stack([
        n1g[0], n1b[0], n2g[0], n2b[0], n1g[1], n1b[1], n2g[1], n2b[1],
        a["conv_b_out"][0], a["ffn_b_down"][0], a["gmlp_b_out"][0], a["ffn_b_down"][1],
        a["gmlp_b_in"][0][D:], a["gmlp_ln_g"][0], a["gmlp_ln_b"][0], a["gmlp_b_s"][0].reshape(-1)]))
    x = a["x"].reshape(SEQ, D)
    arrays = {
        "d_x_tm": np.ascontiguousarray(x),
        "d_x_fm": np.ascontiguousarray(x.reshape(SEQ, KD, P).transpose(2, 1, 0)),
        "d_weights": weights,
        "d_params": params,
        "d_rows": rows,
        "d_spatial": np.ascontiguousarray(a["gmlp_w_s"][0].transpose(2, 0, 1)),
    }
    nc = bacc.Bacc("TRN2", target_bir_lowering=False, num_devices=1)
    args = [nc.dram_tensor(k, v.shape, mybir.dt.from_np(v.dtype), kind="ExternalInput").ap() for k, v in arrays.items()]
    out = nc.dram_tensor("d_out", (SEQ, D), mybir.dt.float32, kind="ExternalOutput").ap()
    build_trunk(nc, *args, out)
    r = run_bass_kernel_spmd(nc, [arrays], core_ids=[0])
    return r.results[0]["d_out"].reshape(1, SEQ, D)
```

```python
import concourse.bass as bass
from concourse import mybir

P = 128
D = 1024
SEQ = 512
DEPTH = 2
NT = SEQ // P
KD = D // P
HID = 2816
KH = HID // P
HALF = 512
TAPS = 31
PAD = TAPS - 1
FTAPS = 3
FPAD = FTAPS - 1
GROUPS = 8
ALPHA = (2.0 * DEPTH) ** 0.25
EPS = 1e-5
UNIT = 1024

U_CONV_IN = 0
U_CONV_OUT = U_CONV_IN + 2 * KD
U_UP0 = U_CONV_OUT + KD
U_DOWN0 = U_UP0 + 2 * KH
U_GV = U_DOWN0 + KH
U_GU = U_GV + KD
U_GOUT = U_GU + KD
U_UP1 = U_GOUT + KD
U_DOWN1 = U_UP1 + 2 * KH
UNITS = U_DOWN1 + KH

RAW = 4
RING = 4
LEAD = 3
X_FIRST = 4
LAST = 4

EARLY = (U_UP0, U_GV, U_UP1)
BEFORE_EARLY = (U_UP0 - 1, U_UP1 - 1)
IS_EARLY = [u in BEFORE_EARLY or any(e <= u < e + RING for e in EARLY) for u in range(UNITS)]
IN_RING = [u for u in range(UNITS) if not IS_EARLY[u]]

PE_TAPS = [10, 10, 11, 11, 10, 11, 11] + [19]
DV_TAPS = [TAPS - n for n in PE_TAPS]
ZC_PARTS = [0, 1, 2, 4, 6, KD]
LAST_AT = 9

C_CIN_B = 0
C_CDW_W = C_CIN_B + 2 * KD
C_CDW_B = C_CDW_W + KD * TAPS
C_CLN_G = C_CDW_B + KD
C_CLN_B = C_CLN_G + KD
C_GU_B = C_CLN_B + KD
C_FUP_B = C_GU_B + KD
C_FDW_W = C_FUP_B + DEPTH * KH * 2
C_FDW_B = C_FDW_W + DEPTH * KH * 2 * FTAPS
NPAR = C_FDW_B + DEPTH * KH * 2

(R_N1G, R_N1B, R_N2G, R_N2B, R_N3G, R_N3B, R_N4G, R_N4B, R_BO1, R_BO2, R_BO3, R_BO4,
 R_GVB, R_GLG, R_GLB, R_GBS, NROW) = range(17)


def build_trunk(nc, x_tm_d, x_fm_d, weights_d, params_d, rows_d, spatial_d, out_d):
    f32 = mybir.dt.float32
    f32r = mybir.dt.float32r
    ALU = mybir.AluOpType
    ACT = mybir.ActivationFunctionType

    base = (nc.sbuf_base + 63) // 64 * 64
    at = [base]

    def place(name, shape, dt, offset=None):
        size = 4
        for n in shape[1:]:
            size *= n
        if offset is None:
            offset = at[0]
            at[0] += (size + 31) // 32 * 32
        return nc.alloc_sbuf_tensor_at(name, shape, dt, offset=offset)

    raw = place("raw", [P, RAW, UNIT], f32)
    wh = place("wh", [P, RING, UNIT], f32r)
    wl = place("wl", [P, RING, UNIT], f32r)
    xh = place("xh", [P, KD, SEQ], f32r)
    xl = place("xl", [P, KD, SEQ], f32r)
    res = place("res", [P, NT, D], f32)
    par = place("par", [P, NPAR], f32)
    brow = place("brow", [P, D], f32)
    ident = place("ident", [P, P], f32)
    half_m = place("half_m", [P, NT], f32)
    spare = place("spare", [P, NT], f32)
    stats = place("stats", [P, NT, 3, 6], f32)
    mv = place("mv", [P, NT, 2], f32)
    veps = place("veps", [P, NT], f32)
    rstd = place("rstd", [P, NT], f32)
    sums = place("sums", [P, NT, 2], f32)
    negm = place("negm", [P, NT], f32)
    sqs = place("sqs", [P, NT], f32)

    s0 = at[0]
    at[0] += 2 * 2080 + 4 * 2048
    grow = place("grow", [P, D], f32, s0)
    brow_n = place("brow_n", [P, D], f32, s0 + 4096)
    bsrow = place("bsrow", [P, GROUPS, P], f32, s0 + 8192)
    gpad = place("gpad", [P, FPAD + SEQ], f32, s0)
    vpad = place("vpad", [P, FPAD + SEQ], f32, s0 + 2080)
    gacc = place("gacc", [P, SEQ], f32, s0 + 4160)
    vacc = place("vacc", [P, SEQ], f32, s0 + 4160 + 2048)
    prod = place("prod", [P, SEQ], f32, s0 + 4160 + 4096)

    h0 = at[0]
    hh = place("hh", [P, KH, SEQ], f32r)
    hl = place("hl", [P, KH, SEQ], f32r)
    assert at[0] <= nc.sbuf_usable_end, (at[0], nc.sbuf_usable_end)
    hend = at[0]
    at[0] = h0
    CW = PAD + SEQ
    xraw = place("xraw", [P, KD, SEQ], f32)
    glu = place("glu", [P, 2, CW], f32)
    gluh = place("gluh", [P, 2, CW], f32r)
    glul = place("glul", [P, 2, CW], f32r)
    sig = place("sig", [P, SEQ], f32)
    a0 = at[0]
    acc = place("acc", [P, 2, SEQ], f32)
    dwh = place("dwh", [P, KD * TAPS], f32r, a0)
    cbuf = place("cbuf", [P, 2, SEQ], f32)
    dwl = place("dwl", [P, KD * TAPS], f32)
    diagh = [place("diagh0", [P, max(PE_TAPS[0::2]), P], f32r),
             place("diagh1", [P, max(PE_TAPS[1::2]), P], f32r, h0)]
    diagl = [place(f"diagl{b}", [P, max(PE_TAPS[b::2]), P], f32r) for b in range(2)]
    ctm = place("ctm", [P, NT, D], f32)
    slb = place("slb", [P, 2, SEQ], f32)
    assert at[0] <= hend
    eh = place("eh", [P, RING, UNIT], f32r, h0 + 4096)
    el = place("el", [P, RING, UNIT], f32r, h0 + 49152)
    bh = place("bh", [P, UNIT], f32r, h0 + 36864)
    bl = place("bl", [P, UNIT], f32r, h0 + 36864 + 4096)
    scaled = place("scaled", [P, D], f32, h0)
    squares = place("squares", [P, D], f32, h0 + 20480)
    wsraw = place("wsraw", [P, GROUPS, P], f32, h0)
    vh = place("vh", [P, NT, D], f32r, h0 + 4096)
    uu = place("uu", [P, KD, SEQ], f32, h0 + 20480)
    gvrow = place("gvrow", [P, D], f32, h0 + 36864)
    glg = place("glg", [P, D], f32, h0 + 36864 + 4096)
    glb = place("glb", [P, D], f32, h0 + 36864 + 8192)
    vl = place("vl", [P, NT, D], f32r, h0 + 49152)
    vtm = place("vtm", [P, NT, D], f32, h0 + 65536)
    wsh = place("wsh", [P, GROUPS, P], f32r, h0 + 81920)
    wsl = place("wsl", [P, GROUPS, P], f32r, h0 + 81920 + 4096)

    ps = nc.alloc_psum_tensor("ps", [P, 8, 512], f32)

    sem = nc.alloc_semaphore
    raw_in = [sem(f"raw_in{i}") for i in range(RAW)]
    xfm_in = [sem(f"xfm_in{i}") for i in range(KD)]
    xtm_in = sem("xtm_in")
    par_in = sem("par_in")
    bo_in = sem("bo_in")
    norm_in = sem("norm_in")
    gv_in = sem("gv_in")
    gm_in = sem("gm_in")
    out_done = sem("out_done")
    const_ok = sem("const_ok")
    w_hi = sem("w_hi")
    w_lo = sem("w_lo")
    w_used = sem("w_used")
    x_hi = sem("x_hi")
    x_lo = sem("x_lo")
    res0_ok = sem("res0_ok")
    res_ok = sem("res_ok")
    res_mul = sem("res_mul")
    dw_ok = sem("dw_ok")
    diag = sem("diag")
    gate_s = sem("gate_s")
    glu_s = sem("glu_s")
    glu_hi = sem("glu_hi")
    glu_lo = sem("glu_lo")
    dw_pe = sem("dw_pe")
    acc_s = sem("acc_s")
    dw_tap = sem("dw_tap")
    conv_c = sem("conv_c")
    ct_pe = sem("ct_pe")
    ct_ok = sem("ct_ok")
    ct_stat = sem("ct_stat")
    zc = sem("zc")
    zt = sem("zt")
    sl = sem("sl")
    blk = sem("blk")
    st_ok = sem("st_ok")
    var_ok = sem("var_ok")
    mean_ok = sem("mean_ok")
    sq_ok = sem("sq_ok")
    eps_ok = sem("eps_ok")
    rstd_ok = sem("rstd_ok")
    nrm = sem("nrm")
    x_ok = sem("x_ok")
    xt = sem("xt")
    g_in = sem("g_in")
    v_in = sem("v_in")
    tap = sem("tap")
    PAD_TAPS = 2 * 2 * FTAPS
    gs = sem("gs")
    pr = sem("pr")
    h_hi = sem("h_hi")
    h_lo = sem("h_lo")
    v_ev = sem("v_ev")
    v_gelu = sem("v_gelu")
    u_gelu = sem("u_gelu")
    v_n = sem("v_n")
    v_hi = sem("v_hi")
    v_lo = sem("v_lo")
    ws_m = sem("ws_m")
    ws_hi = sem("ws_hi")
    ws_lo = sem("ws_lo")
    sp = sem("sp")
    sp_b = sem("sp_b")
    us_s = sem("us_s")
    us_hi = sem("us_hi")
    us_lo = sem("us_lo")

    blk_of = [0, NT - 1, 3 * (NT - 1), 4 * (NT - 1)]
    X0 = KD
    XC = X0 + KD
    XN = [XC + 2 * NT * (n + 1) for n in range(3)]
    B0 = [0, 0, 4, 4]
    B1 = [4, 4, 0, 0]

    def split_at(u):
        if u in BEFORE_EARLY:
            return bh[:, :], bl[:, :]
        if IS_EARLY[u]:
            q = (u - max(e for e in EARLY if e <= u)) % RING
            return eh[:, q, :], el[:, q, :]
        q = IN_RING.index(u) % RING
        return wh[:, q, :], wl[:, q, :]

    def wait_split(eng, u):
        if u == BEFORE_EARLY[0]:
            eng.wait_ge(conv_c, KD)
        elif u == BEFORE_EARLY[1]:
            eng.wait_ge(v_n, NT)
        elif u == U_GV:
            eng.wait_ge(w_used, U_GV - LAST)
        elif u == U_UP1:
            eng.wait_ge(sp, GROUPS)
        elif not IS_EARLY[u] and IN_RING.index(u) >= RING:
            eng.wait_ge(w_used, IN_RING[IN_RING.index(u) - RING] + 1)

    block = nc.Block()
    block.__enter__()

    @block.sync
    def _(eng):
        def load(slot, unit):
            eng.dma_start(raw[:, slot, :], weights_d[bass.ds(unit, 1), :, :].rearrange("o p n -> p (o n)")
                          ).then_inc(raw_in[slot], 16)

        load(0, 0)
        for k in range(KD):
            if k == X_FIRST:
                load(1, 1)
            eng.dma_start(xraw[:, k, :], x_fm_d[:, k, :]).then_inc(xfm_in[k], 16)
        eng.dma_start(par[:, :], params_d).then_inc(par_in, 16)
        load(2, 2)
        load(3, 3)
        for u in range(RAW, 2 * RAW):
            eng.wait_ge(w_lo, u - RAW + 1)
            load(u - RAW, u)
            t = u - RAW
            eng.dma_start(res[:, t, :], x_tm_d[t * P:(t + 1) * P, :]).then_inc(xtm_in, 16)
        eng.dma_start(brow[:, :], rows_d[R_BO1:R_BO1 + 1, :].partition_broadcast(P)).then_inc(bo_in, 16)
        eng.dma_start(grow[:, :], rows_d[R_N1G:R_N1G + 1, :].partition_broadcast(P)).then_inc(norm_in, 16)
        eng.dma_start(brow_n[:, :], rows_d[R_N1B:R_N1B + 1, :].partition_broadcast(P)).then_inc(norm_in, 16)
        with eng.Fori(2, UNITS // RAW) as i:
            for s in range(RAW):
                eng.wait_ge(w_lo, i * RAW + (s - RAW + 1))
                load(s, i * RAW + s)
        for t in range(NT):
            eng.wait_ge(x_ok, 3 * NT + t + 1)
            if t < NT - 1:
                eng.dma_start(out_d[t * P:(t + 1) * P, :], res[:, t, :]).then_inc(out_done, 16)
        eng.dma_start(out_d[SEQ - P:SEQ, 0:HALF], res[:, NT - 1, 0:HALF]).then_inc(out_done, 16)
        eng.wait_ge(x_ok, 4 * NT + 1)
        eng.dma_start(out_d[SEQ - P:SEQ, HALF:D], res[:, NT - 1, HALF:D]).then_inc(out_done, 16)
        eng.wait_ge(out_done, 16 * (NT + 1))

    @block.gpsimd
    def _(eng):
        def root(k, t, n):
            eng.wait_ge(eps_ok, k + 1)
            eng.tensor_tensor(rstd[:, t:t + n], veps[:, t:t + n], half_m[:, t:t + n], ALU.pow).then_inc(rstd_ok, 1)

        def mixer_root(k, seen, t, n):
            eng.wait_ge(var_ok, seen)
            eng.tensor_scalar(veps[:, t:t + n], mv[:, t:t + n, 1], EPS, None, ALU.add).then_inc(eps_ok, 1)
            root(k, t, n)

        def norm_root(k, seen, t):
            eng.wait_ge(sq_ok, seen)
            eng.tensor_scalar(veps[:, t:t + 1], sqs[:, t:t + 1], 1.0 / D, EPS, ALU.mult, ALU.add).then_inc(eps_ok, 1)
            root(k, t, 1)

        eng.memset(half_m[:, :], -0.5).then_inc(const_ok, 1)
        eng.memset(ident[:, :], 0.0).then_inc(const_ok, 1)
        eng.wait_ge(const_ok, 2)
        eng.affine_select(out=ident[:, :], in_=ident[:, :], compare_op=ALU.not_equal, fill=1.0, base=0,
                          pattern=[[-1, P]], channel_multiplier=1).then_inc(const_ok, 1)
        eng.wait_ge(xtm_in, 16 * NT)
        eng.wait_ge(bo_in, 16)
        for t in range(NT):
            eng.tensor_scalar(res[:, t, :], res[:, t, :], ALPHA, None, ALU.mult).then_inc(res_mul, 1)
            eng.wait_ge(res_mul, t + 1)
            eng.tensor_tensor(res[:, t, :], res[:, t, :], brow[:, :], ALU.add).then_inc(res0_ok, 1)

        mixer_root(0, 1, 0, NT)
        for n in range(2):
            for t in range(NT):
                norm_root(1 + n * NT + t, n * NT + t + 1, t)
        eng.wait_ge(gm_in, 16 * 4)
        eng.affine_select(out=wsraw[:, :, :], in_=wsraw[:, :, :], compare_op=ALU.is_ge, fill=0.0,
                          base=0, pattern=[[0, GROUPS], [1, P]], channel_multiplier=-1).then_inc(ws_m, 1)
        for t in range(NT):
            mixer_root(1 + 2 * NT + t, t + 2, t, 1)
        for n in range(2, 4):
            for t in range(NT):
                norm_root(1 + (n + 1) * NT + t, n * NT + t + 1, t)

    @block.scalar
    def _(eng):
        def his(units):
            for u in units:
                if u < UNITS:
                    wait_split(eng, u)
                    eng.wait_ge(raw_in[u % RAW], 16 + u // RAW * 16)
                    eng.activation(split_at(u)[0], raw[:, u % RAW, :], ACT.Copy).then_inc(w_hi, 1)

        def row(dst, r, s):
            eng.dma_start(dst, rows_d[r:r + 1, :].partition_broadcast(P)).then_inc(s, 16)

        def table_of(func):
            eng.activation(spare[:, :], half_m[:, :], func)

        eng.wait_ge(const_ok, 1)

        def norm_rows(n):
            row(grow[:, :], R_N1G + 2 * n, norm_in)
            row(brow_n[:, :], R_N1B + 2 * n, norm_in)

        table_of(ACT.Sigmoid)
        his([0])
        for k in range(KD):
            eng.wait_ge(xfm_in[k], 16)
            eng.activation(xh[:, k, :], xraw[:, k, :], ACT.Copy).then_inc(x_hi, 1)
            if k == X_FIRST:
                his([1])
        his(range(2, LEAD + 1))
        eng.wait_ge(par_in, 16)
        eng.wait_ge(const_ok, 3)

        def diagonals(j, part=None):
            n = PE_TAPS[j]
            if j == 0:
                eng.wait_ge(dw_ok, 2)
            if j >= 2:
                eng.wait_ge(dw_pe, j - 1)
            for q in (range(n), range(n // 2), range(n // 2, n))[0 if part is None else 1 + part]:
                c = j * TAPS + DV_TAPS[j] + q
                eng.activation(diagh[j % 2][:, q, :], ident[:, :], ACT.Copy, scale=par[:, C_CDW_W + c:C_CDW_W + c + 1])
                last = eng.activation(diagl[j % 2][:, q, :], ident[:, :], ACT.Copy, scale=dwl[:, c:c + 1])
            if part != 0:
                last.then_inc(diag, 1)

        def first_taps(j):
            if j > 0:
                eng.wait_ge(conv_c, j)
            c = C_CDW_W + j * TAPS
            eng.activation(acc[:, 0, :], glu[:, j % 2, 0:SEQ], ACT.Identity, scale=par[:, c:c + 1],
                           bias=par[:, C_CDW_B + j:C_CDW_B + j + 1]).then_inc(acc_s, 1)
            eng.activation(acc[:, 1, :], glu[:, j % 2, 1:1 + SEQ], ACT.Copy, scale=par[:, c + 1:c + 2]).then_inc(acc_s, 1)

        def ct_out(j):
            eng.wait_ge(ct_pe, j + 1)
            eng.activation(ctm[:, :, j * P:(j + 1) * P],
                           ps[:, 6 + j % 2, :].rearrange("p (t n) -> p t n", t=NT), ACT.Copy).then_inc(ct_ok, 1)

        diagonals(0, 0)
        for j in range(KD):
            if 0 < j < KD - 1:
                his([2 * j + LEAD])
            eng.wait_ge(w_used, 2 * j + 1)
            if j >= 1:
                eng.wait_ge(glu_s, j)
            b = C_CIN_B + KD + j
            eng.activation(sig[:, :], ps[:, 2 * j % 4, :], ACT.Sigmoid, bias=par[:, b:b + 1]).then_inc(gate_s, 1)
            if 0 < j < KD - 1:
                his([2 * j + 1 + LEAD])
            eng.wait_ge(glu_s, j + 1)
            if j >= 2:
                eng.wait_ge(dw_pe, j - 1)
            eng.activation(gluh[:, j % 2, PAD:CW], glu[:, j % 2, PAD:CW], ACT.Copy).then_inc(glu_hi, 1)
            if j < KD - 1:
                first_taps(j)
            if j in (0, KD - 1):
                diagonals(j, 1)
            if j == 0:
                his([1 + LEAD])
            if j >= 2:
                ct_out(j - 2)
            if j == KD - 1:
                first_taps(j)
            if j + 1 < KD - 1:
                diagonals(j + 1)
            elif j + 1 == KD - 1:
                diagonals(j + 1, 0)
        his([U_CONV_OUT + 1, U_CONV_OUT + 2])
        eng.wait_ge(res0_ok, NT)
        row(brow[:, :], R_BO2, bo_in)
        ct_out(KD - 2)
        table_of(ACT.Silu)
        eng.wait_ge(ct_stat, 1)
        ct_out(KD - 1)

        ahead = {2: U_CONV_OUT + 3, 3: U_CONV_OUT + 4, 5: U_CONV_OUT + 5, 7: U_CONV_OUT + 6}
        for k in range(KD):
            eng.wait_ge(zt, k + 1)
            if k >= 2:
                eng.wait_ge(x_lo, X0 + k - 1)
            eng.activation(slb[:, k % 2, :], ps[:, 4 + k % 2, :], ACT.Silu, scale=par[:, C_CLN_G + k:C_CLN_G + k + 1],
                           bias=par[:, C_CLN_B + k:C_CLN_B + k + 1]).then_inc(sl, 1)
            eng.wait_ge(sl, k + 1)
            eng.activation(xh[:, k, :], slb[:, k % 2, :], ACT.Copy).then_inc(x_hi, 1)
            if k in ahead:
                his([ahead[k]])
        his(range(U_CONV_OUT + 7, U_UP0 + 2))

        def squared(n, t):
            eng.wait_ge(mean_ok, n * NT + t + 1)
            eng.activation(squares[:, :], res[:, t, :], ACT.Square, bias=negm[:, t:t + 1],
                           accum_out=sqs[:, t:t + 1]).then_inc(sq_ok, 1)

        def block_hi(n, t, q):
            eng.wait_ge(xt, 2 * (n * NT + t) + q + 1)
            eng.activation(xh[:, 4 * q:4 * q + 4, t * P:(t + 1) * P],
                           ps[:, B0[n] + 2 * (t % 2) + q, :].rearrange("p (k n) -> p k n", k=4), ACT.Copy).then_inc(x_hi, 1)

        def norm(n):
            for t in range(NT):
                if n < 3 and t > 0:
                    block_hi(n, t - 1, 0)
                squared(n, t)
                if n < 3:
                    if t > 0:
                        block_hi(n, t - 1, 1)
                    if t in (0, 2):
                        his([EARLY[n] + 2 + t // 2])
            if n < 3:
                block_hi(n, NT - 1, 0)
                block_hi(n, NT - 1, 1)

        def ffn_up(layer, u0, bank0):
            first_tap = PAD_TAPS * (layer + 1) + 6 * KH * layer
            slot0 = IN_RING.index(u0 + RING) % RING

            def tile(i, q, ahead):
                pair = i * 2 + q
                done = first_tap + 6 * q
                ahead(2 * q)
                for v, (buf, signal) in enumerate(((gpad, g_in), (vpad, v_in))):
                    eng.wait_ge(w_used, i * 4 + (u0 + 2 * q + v + 1))
                    eng.wait_ge(tap, i * 12 + (done - 3 + 3 * v))
                    c = pair * 2 + (C_FUP_B + 2 * KH * layer + v)
                    eng.activation(buf[:, FPAD:], ps[:, bank0 + 2 * q + v, :], ACT.Identity,
                                   bias=par[:, bass.ds(c, 1)]).then_inc(signal, 1)
                    if v == 0:
                        ahead(2 * q + 1)
                eng.wait_ge(tap, i * 12 + (done + 3))
                eng.activation(gacc[:, :], gacc[:, :], ACT.Silu).then_inc(gs, 1)
                eng.wait_ge(pr, pair + (layer * KH + 1))
                eng.activation(hh[:, bass.ds(pair, 1), :].rearrange("p o n -> p (o n)"), prod[:, :], ACT.Copy).then_inc(h_hi, 1)

            for q in range(2):
                tile(0, q, lambda c: his([u0 + c + LEAD] if c else []))
            with eng.Fori(1, KH // 2) as i:
                def ahead(c):
                    slot, part = (slot0 + c + LEAD) % RING, (u0 + c + LEAD) % RAW
                    eng.wait_ge(w_used, i * 4 + (u0 + c + LEAD - RING + 1))
                    eng.wait_ge(raw_in[part], i * 16 + 16 * ((u0 + c + LEAD) // RAW + 1))
                    eng.activation(wh[:, slot, :], raw[:, part, :], ACT.Copy).then_inc(w_hi, 1)
                for q in range(2):
                    tile(i, q, ahead)

        norm(0)
        ffn_up(0, U_UP0, 4)
        eng.wait_ge(res_ok, NT)
        row(brow[:, :], R_BO3, bo_in)
        eng.wait_ge(h_lo, KH)
        norm_rows(1)
        his(range(U_DOWN0 + LEAD, U_GV + 2))
        norm(1)

        eng.wait_ge(w_used, U_GV)
        row(gvrow[:, :], R_GVB, gv_in)
        row(glg[:, :], R_GLG, gm_in)
        row(glb[:, :], R_GLB, gm_in)
        eng.wait_ge(x_ok, 2 * NT)
        eng.dma_start(wsraw[:, :, :], spatial_d).then_inc(gm_in, 16)
        row(bsrow[:, :, :].rearrange("p g t -> p (g t)"), R_GBS, gm_in)
        norm_rows(2)
        for h in range(2):
            for t in range(NT):
                eng.wait_ge(v_ev, h * NT + t + 1)
                eng.activation(vtm[:, t, h * HALF:(h + 1) * HALF], vtm[:, t, h * HALF:(h + 1) * HALF], ACT.Gelu).then_inc(v_gelu, 1)
                if h == 0:
                    his([U_GV + 4 + t])
            if h == 0:
                his(range(U_GU, U_GU + LEAD))
        his([U_GU + LEAD])
        eng.wait_ge(ws_m, 1)
        eng.activation(wsh[:, :, :], wsraw[:, :, :], ACT.Copy).then_inc(ws_hi, 1)
        def gelu_u(j):
            eng.wait_ge(w_used, U_GU + j + 1)
            eng.activation(uu[:, j, :], ps[:, 4 + j % 4, :], ACT.Gelu, bias=par[:, C_GU_B + j:C_GU_B + j + 1]).then_inc(u_gelu, 1)

        for j in range(KD - 1):
            gelu_u(j)
            his([U_GU + 4 + j])
            if j < NT:
                eng.wait_ge(v_n, j + 1)
                eng.activation(vh[:, j, :], vtm[:, j, :], ACT.Copy).then_inc(v_hi, 1)
        eng.wait_ge(res_ok, 2 * NT)
        row(brow[:, :], R_BO4, bo_in)
        for g in range(GROUPS):
            eng.wait_ge(us_s, g + 1)
            if g == 0:
                eng.wait_ge(w_used, U_GU + KD)
            eng.activation(xh[:, g, :], uu[:, g, :], ACT.Copy).then_inc(us_hi, 1)
            if g == 0:
                gelu_u(KD - 1)
            if g == 1:
                his([U_GOUT + 3])
            if g % 2 and g >= 3:
                his([U_GOUT + 4 + (g - 3) // 2])
        his(range(U_GOUT + 7, U_UP1 + 2))
        norm(2)
        ffn_up(1, U_UP1, 0)
        eng.wait_ge(h_lo, 2 * KH)
        norm_rows(3)
        his(range(U_DOWN1 + LEAD, UNITS))
        norm(3)

    @block.vector
    def _(eng):
        def los(units):
            for u in units:
                if u < UNITS:
                    wait_split(eng, u)
                    eng.wait_ge(w_hi, u + 1)
                    h, l = split_at(u)
                    eng.tensor_tensor(l, raw[:, u % RAW, :], h.bitcast(f32), ALU.subtract).then_inc(w_lo, 1)

        seq = [0]

        def stat(ins):
            seq[0] += 1
            ins.then_inc(st_ok, 1)
            return seq[0]

        eng.memset(glu[:, :, 0:PAD], 0.0).then_inc(dw_ok, 1)
        eng.memset(gluh[:, :, 0:PAD].bitcast(f32), 0.0)
        eng.memset(glul[:, :, 0:PAD].bitcast(f32), 0.0)
        los([0])
        for k in range(KD):
            eng.wait_ge(x_hi, k + 1)
            eng.tensor_tensor(xl[:, k, :], xraw[:, k, :], xh[:, k, :].bitcast(f32), ALU.subtract).then_inc(x_lo, 1)
            if k == X_FIRST:
                los([1])
        eng.wait_ge(par_in, 16)
        n = stat(eng.tensor_copy(dwh[:, :], par[:, C_CDW_W:C_CDW_W + KD * TAPS]))
        eng.wait_ge(st_ok, n)
        eng.tensor_tensor(dwl[:, :], par[:, C_CDW_W:C_CDW_W + KD * TAPS], dwh[:, :].bitcast(f32), ALU.subtract).then_inc(dw_ok, 1)
        los([2])

        def gated_channels(j):
            eng.wait_ge(gate_s, j + 1)
            eng.wait_ge(w_used, 2 * j + 2)
            eng.scalar_tensor_tensor(out=glu[:, j % 2, PAD:CW], in0=ps[:, (2 * j + 1) % 4, :], scalar=par[:, C_CIN_B + j:C_CIN_B + j + 1],
                                     in1=sig[:, :], op0=ALU.add, op1=ALU.mult).then_inc(glu_s, 1)

        def gated_low(j):
            eng.wait_ge(glu_hi, j + 1)
            eng.tensor_tensor(glul[:, j % 2, PAD:CW], glu[:, j % 2, PAD:CW], gluh[:, j % 2, PAD:CW].bitcast(f32),
                              ALU.subtract).then_inc(glu_lo, 1)

        taps_before = 0
        for j in range(KD):
            if j < KD - 1:
                los([2 * j + LEAD])
                gated_channels(j)
                if j > 0:
                    los([2 * j + 1 + LEAD])
                gated_low(j)
            for k in range(2, DV_TAPS[j]):
                c = C_CDW_W + j * TAPS + k
                if j == 0 and k == 10:
                    los([1 + LEAD])
                if j == KD - 2 and k == LAST_AT:
                    gated_channels(KD - 1)
                if j == KD - 2 and k == LAST_AT + 2:
                    gated_low(KD - 1)
                if k < 4:
                    eng.wait_ge(acc_s, 2 * j + k - 1)
                else:
                    eng.wait_ge(dw_tap, taps_before + k - 3)
                eng.scalar_tensor_tensor(out=acc[:, k % 2, :], in0=glu[:, j % 2, k:k + SEQ], scalar=par[:, c:c + 1],
                                         in1=acc[:, k % 2, :], op0=ALU.mult, op1=ALU.add).then_inc(dw_tap, 1)
            taps_before += DV_TAPS[j] - 2
            if j == 5:
                eng.wait_ge(ct_ok, 4)
                for t in range(NT):
                    stat(eng.bn_stats(stats[:, t, 0, :], ctm[:, t, 0:HALF]))
            if j == KD - 1:
                eng.wait_ge(ct_ok, KD - 1)
                for t in range(NT):
                    stat(eng.bn_stats(stats[:, t, 1, :], ctm[:, t, HALF:D - P]))
            eng.wait_ge(dw_tap, taps_before)
            n = stat(eng.tensor_tensor(acc[:, 0, :], acc[:, 0, :], acc[:, 1, :], ALU.add))
            eng.wait_ge(st_ok, n)
            eng.wait_ge(dw_pe, j + 1)
            if j >= 2:
                eng.wait_ge(ct_pe, j - 1)
            eng.tensor_tensor(cbuf[:, j % 2, :], acc[:, 0, :], ps[:, 4 + j % 2, :], ALU.add).then_inc(conv_c, 1)
        eng.wait_ge(ct_pe, KD)
        for t in range(NT):
            ins = eng.bn_stats(stats[:, t, 2, :], ps[:, 6 + (KD - 1) % 2, t * P:(t + 1) * P])
        ins.then_inc(ct_stat, 1)
        eng.wait_ge(ct_stat, 1)
        for t in range(NT):
            ins = eng.bn_aggr(mv[:, t, :], stats[:, t, :, :].rearrange("p a b -> p (a b)"))
        ins.then_inc(var_ok, 1)
        los([U_CONV_OUT + 1])
        eng.wait_ge(var_ok, 1)
        eng.wait_ge(rstd_ok, 1)
        eng.wait_ge(ct_ok, KD)

        def normalized(part):
            for t in range(NT):
                c = ctm[:, t, ZC_PARTS[part] * P:ZC_PARTS[part + 1] * P]
                eng.tensor_scalar(c, c, mv[:, t, 0:1], rstd[:, t:t + 1], ALU.subtract, ALU.mult).then_inc(zc, 1)
        for part in range(3):
            normalized(part)
        ahead = {2: U_CONV_OUT + 3, 3: U_CONV_OUT + 4, 5: U_CONV_OUT + 5, 7: U_CONV_OUT + 6}
        for k in range(KD):
            eng.wait_ge(x_hi, X0 + k + 1)
            eng.tensor_tensor(xl[:, k, :], slb[:, k % 2, :], xh[:, k, :].bitcast(f32), ALU.subtract).then_inc(x_lo, 1)
            if k < 2:
                normalized(3 + k)
            if k == 2:
                los([U_CONV_OUT + 2])
            if k in ahead:
                los([ahead[k]])
        los(range(U_CONV_OUT + 7, U_UP0 + 2))

        def half_sum(n, t, h):
            r = res[:, t, h * HALF:(h + 1) * HALF]
            bank = (B1 if h else B0)[n] + t
            return stat(eng.scalar_tensor_tensor(out=r, in0=ps[:, bank, :], scalar=1.0, in1=r, op0=ALU.mult, op1=ALU.add,
                                                 accum_out=sums[:, t, h:h + 1]))

        def first_halves(n, u_half):
            eng.wait_ge(w_used, u_half)
            if n == 0:
                eng.wait_ge(res0_ok, NT)
            for t in range(NT):
                half_sum(n, t, 0)

        def second_half(n, t, u_end):
            if t < NT - 1:
                eng.wait_ge(blk, blk_of[n] + t + 1)
            else:
                eng.wait_ge(w_used, u_end)
            eng.wait_ge(st_ok, half_sum(n, t, 1))
            eng.tensor_scalar(negm[:, t:t + 1], sums[:, t, 0:1], sums[:, t, 1:2], -1.0 / D, ALU.add, ALU.mult).then_inc(mean_ok, 1)
            if t == 0:
                eng.wait_ge(norm_in, 32 * (n + 1))
            eng.wait_ge(mean_ok, n * NT + t + 1)
            eng.scalar_tensor_tensor(out=scaled[:, :], in0=res[:, t, :], scalar=negm[:, t:t + 1], in1=grow[:, :],
                                     op0=ALU.add, op1=ALU.mult).then_inc(nrm, 1)
            if n < 3 and t > 0:
                block_lo(n, t - 1)
            eng.wait_ge(nrm, n * NT + t + 1)
            eng.wait_ge(rstd_ok, 1 + n * NT + t + 1 + (NT if n >= 2 else 0))
            last = n == 3 and t == NT - 1
            for c in ((slice(0, HALF), slice(HALF, D)) if last else (slice(0, D),)):
                eng.scalar_tensor_tensor(out=res[:, t, c], in0=scaled[:, c], scalar=rstd[:, t:t + 1], in1=brow_n[:, c],
                                         op0=ALU.mult, op1=ALU.add).then_inc(x_ok, 1)

        def block_lo(n, t):
            for q in range(2):
                eng.wait_ge(x_hi, XC + n * 2 * NT + 2 * t + q + 1)
                eng.tensor_tensor(xl[:, 4 * q:4 * q + 4, t * P:(t + 1) * P],
                                  ps[:, B0[n] + 2 * (t % 2) + q, :].rearrange("p (k n) -> p k n", k=4),
                                  xh[:, 4 * q:4 * q + 4, t * P:(t + 1) * P].bitcast(f32), ALU.subtract).then_inc(x_lo, 1)

        def norm(n, u_end):
            for t in range(NT):
                second_half(n, t, u_end)
                if n < 3 and t in (0, 2):
                    los([EARLY[n] + 2 + t // 2])
            if n < 3:
                block_lo(n, NT - 1)

        def residual(n):
            eng.wait_ge(bo_in, 16 * (n + 1))
            for t in range(NT):
                eng.scalar_tensor_tensor(out=res[:, t, :], in0=res[:, t, :], scalar=ALPHA, in1=brow[:, :],
                                         op0=ALU.mult, op1=ALU.add).then_inc(res_ok, 1)

        def ffn_up(layer, u0):
            slot0 = IN_RING.index(u0 + RING) % RING
            first_tap = PAD_TAPS * (layer + 1) + 6 * KH * layer
            eng.wait_ge(x_ok, (2 * layer + 1) * NT)
            eng.memset(gpad[:, 0:FPAD], 0.0).then_inc(tap, PAD_TAPS // 2)
            eng.memset(vpad[:, 0:FPAD], 0.0).then_inc(tap, PAD_TAPS // 2)
            eng.wait_ge(tap, first_tap)

            def tile(i, q, ahead):
                pair = i * 2 + q
                done = first_tap + 6 * q
                ahead(2 * q)
                for v, (buf, sums_v, signal) in enumerate(((gpad, gacc, g_in), (vpad, vacc, v_in))):
                    eng.wait_ge(signal, pair + (layer * KH + 1))
                    cb = pair * 2 + (C_FDW_B + 2 * KH * layer + v)
                    for k in range(FTAPS):
                        cw = pair * (2 * FTAPS) + (C_FDW_W + FTAPS * (2 * KH * layer + v) + FTAPS - 1 - k)
                        off = FPAD - k
                        if k == 0:
                            eng.tensor_scalar(sums_v[:, :], buf[:, off:off + SEQ], par[:, bass.ds(cw, 1)], par[:, bass.ds(cb, 1)],
                                              ALU.mult, ALU.add).then_inc(tap, 1)
                        else:
                            eng.wait_ge(tap, i * 12 + (done + 3 * v + k))
                            eng.scalar_tensor_tensor(out=sums_v[:, :], in0=buf[:, off:off + SEQ], scalar=par[:, bass.ds(cw, 1)],
                                                     in1=sums_v[:, :], op0=ALU.mult, op1=ALU.add).then_inc(tap, 1)
                eng.wait_ge(tap, i * 12 + (done + 6))
                eng.wait_ge(gs, pair + (layer * KH + 1))
                eng.tensor_tensor(prod[:, :], gacc[:, :], vacc[:, :], ALU.mult).then_inc(pr, 1)
                ahead(2 * q + 1)
                eng.wait_ge(h_hi, pair + (layer * KH + 1))
                eng.tensor_tensor(hl[:, bass.ds(pair, 1), :].rearrange("p o n -> p (o n)"), prod[:, :],
                                  hh[:, bass.ds(pair, 1), :].rearrange("p o n -> p (o n)").bitcast(f32), ALU.subtract).then_inc(h_lo, 1)

            for q in range(2):
                tile(0, q, lambda c: los([u0 + c + LEAD] if c else []))
            residual(2 * layer + 1)
            with eng.Fori(1, KH // 2) as i:
                def ahead(c):
                    slot, part = (slot0 + c + LEAD) % RING, (u0 + c + LEAD) % RAW
                    eng.wait_ge(w_hi, i * 4 + (u0 + c + LEAD + 1))
                    eng.tensor_tensor(wl[:, slot, :], raw[:, part, :], wh[:, slot, :].bitcast(f32), ALU.subtract).then_inc(w_lo, 1)
                for q in range(2):
                    tile(i, q, ahead)

        def ffn_down(n, u0):
            los(range(u0 + LEAD, u0 + KH // 2 + RING))
            first_halves(n, u0 + KH // 2)
            los(range(u0 + KH // 2 + RING, u0 + KH + (2 if n < 3 else 0)))
            norm(n, u0 + KH)

        first_halves(0, U_CONV_OUT + 4)
        norm(0, U_UP0)
        ffn_up(0, U_UP0)
        ffn_down(1, U_DOWN0)

        eng.wait_ge(gv_in, 16)
        for h in range(2):
            for t in range(NT):
                if h == 0 and t < NT - 1:
                    eng.wait_ge(blk, 2 * (NT - 1) + t + 1)
                else:
                    eng.wait_ge(w_used, U_GV + 4 * (h + 1))
                cols = slice(h * HALF, (h + 1) * HALF)
                eng.tensor_tensor(vtm[:, t, cols], ps[:, 4 - 4 * h + t, :], gvrow[:, cols], ALU.add).then_inc(v_ev, 1)
                if h == 0:
                    los([U_GV + 4 + t])
                if t >= 1:
                    eng.wait_ge(v_gelu, h * NT + t)
                    stat(eng.bn_stats(stats[:, t - 1, h, :], vtm[:, t - 1, cols]))
            eng.wait_ge(v_gelu, (h + 1) * NT)
            n = stat(eng.bn_stats(stats[:, NT - 1, h, :], vtm[:, NT - 1, cols]))
            if h == 0:
                los([U_GU])
                residual(2)
                los([U_GU + 1, U_GU + 2])
        los([U_GU + LEAD])
        eng.wait_ge(st_ok, n)
        for t in range(NT):
            eng.bn_aggr(mv[:, t, :], stats[:, t, 0:2, :].rearrange("p a b -> p (a b)")).then_inc(var_ok, 1)
        eng.wait_ge(gm_in, 16 * 4)
        for t in range(NT):
            eng.wait_ge(var_ok, t + 2)
            k = stat(eng.scalar_tensor_tensor(out=vtm[:, t, :], in0=vtm[:, t, :], scalar=mv[:, t, 0:1], in1=glg[:, :],
                                              op0=ALU.subtract, op1=ALU.mult))
            eng.wait_ge(st_ok, k)
            eng.wait_ge(rstd_ok, 1 + 2 * NT + t + 1)
            eng.scalar_tensor_tensor(out=vtm[:, t, :], in0=vtm[:, t, :], scalar=rstd[:, t:t + 1], in1=glb[:, :],
                                     op0=ALU.mult, op1=ALU.add).then_inc(v_n, 1)
            los([U_GU + 4 + t])
            eng.wait_ge(v_hi, t + 1)
            eng.tensor_tensor(vl[:, t, :], vtm[:, t, :], vh[:, t, :].bitcast(f32), ALU.subtract).then_inc(v_lo, 1)
            if t == 0:
                eng.wait_ge(ws_hi, 1)
                eng.tensor_tensor(wsl[:, :, :], wsraw[:, :, :], wsh[:, :, :].bitcast(f32), ALU.subtract).then_inc(ws_lo, 1)

        def gated(g):
            eng.wait_ge(sp, g + 1)
            bias = bsrow[:, g:g + 1, :].broadcast_to([P, NT, P])
            s_g = ps[:, g % 4, :].rearrange("p (n t) -> p n t", n=NT)
            eng.tensor_tensor(s_g, s_g, bias, ALU.add).then_inc(sp_b, 1)
            eng.wait_ge(sp_b, g + 1)
            eng.wait_ge(u_gelu, g + 1)
            eng.tensor_tensor(uu[:, g, :], ps[:, g % 4, :], uu[:, g, :], ALU.mult).then_inc(us_s, 1)

        los(range(U_GU + 8, U_GU + 10))
        gated(0)
        gated(1)
        los([U_GU + 10])
        for g in range(GROUPS):
            eng.wait_ge(us_hi, g + 1)
            eng.tensor_tensor(xl[:, g, :], uu[:, g, :], xh[:, g, :].bitcast(f32), ALU.subtract).then_inc(us_lo, 1)
            if g + 2 < GROUPS:
                gated(g + 2)
            if g == 1:
                los([U_GOUT + 3])
            if g % 2 and g >= 3:
                los([U_GOUT + 4 + (g - 3) // 2])
        los(range(U_GOUT + 7, U_UP1 + 2))
        first_halves(2, U_GOUT + 4)
        norm(2, U_UP1)
        ffn_up(1, U_UP1)
        ffn_down(3, U_DOWN1)

    @block.tensor
    def _(eng):
        def up(w, bank, cols=slice(0, SEQ), tiles=range(KD)):
            w_h, w_l = w
            for k in tiles:
                a, b = w_h[:, k * P:(k + 1) * P], w_l[:, k * P:(k + 1) * P]
                eng.matmul(ps[:, bank, cols], a, xh[:, k, cols], start=(k == 0), stop=False)
                eng.matmul(ps[:, bank, cols], a, xl[:, k, cols], start=False, stop=False)
                mm = eng.matmul(ps[:, bank, cols], b, xh[:, k, cols], start=False, stop=(k == KD - 1))
            return mm

        def down(u, c, t, bank, st_h, st_l, k, first, last):
            h, l = split_at(u)
            w_h, w_l = h[:, c * HALF:(c + 1) * HALF], l[:, c * HALF:(c + 1) * HALF]
            s_h, s_l = st_h[:, k, t * P:(t + 1) * P], st_l[:, k, t * P:(t + 1) * P]
            eng.matmul(ps[:, bank + t, :], s_h, w_h, start=first, stop=False)
            eng.matmul(ps[:, bank + t, :], s_h, w_l, start=False, stop=False)
            return eng.matmul(ps[:, bank + t, :], s_l, w_h, start=False, stop=last)

        def down_by_k(u0, n, bank, st_h, st_l, k0, kn, before=None):
            for i in range(n):
                eng.wait_ge(w_lo, u0 + i + 1)
                for c in range(2):
                    k = k0 + 2 * i + c
                    if before is not None:
                        before(k)
                    for t in range(NT):
                        mm = down(u0 + i, c, t, bank, st_h, st_l, k, k == 0, k == kn - 1)
                mm.then_inc(w_used, 1)

        def down_by_block(u0, n, bank, st_h, st_l, k0, kn, after, before=None):
            for t in range(NT):
                if before is not None:
                    before(t)
                for i in range(n):
                    if t == 0:
                        eng.wait_ge(w_lo, u0 + i + 1)
                    for c in range(2):
                        k = k0 + 2 * i + c
                        mm = down(u0 + i, c, t, bank, st_h, st_l, k, k == 0, k == kn - 1)
                    if t == NT - 1:
                        mm.then_inc(w_used, 1)
                if t < NT - 1:
                    mm.then_inc(blk, 1)
                after(t)

        def unit_conv(u):
            j = u // 2
            eng.wait_ge(w_lo, u + 1)
            if j >= 2:
                eng.wait_ge(glu_s if u % 2 else gate_s, j - 1)
            up(split_at(u), u % 4).then_inc(w_used, 1)

        def first_units():
            eng.wait_ge(w_lo, 1)
            for k in range(X_FIRST + 1):
                eng.wait_ge(x_lo, k + 1)
                up(split_at(0), 0, tiles=[k])
            eng.wait_ge(w_lo, 2)
            up(split_at(1), 1, tiles=range(X_FIRST))
            for k in range(X_FIRST + 1, KD):
                eng.wait_ge(x_lo, k + 1)
                mm = up(split_at(0), 0, tiles=[k])
            mm.then_inc(w_used, 1)
            up(split_at(1), 1, tiles=range(X_FIRST, KD)).then_inc(w_used, 1)

        def taps(j, amid=None):
            eng.wait_ge(glu_lo, j + 1)
            eng.wait_ge(diag, j + 1)
            if j >= 2:
                eng.wait_ge(conv_c, j - 1)
            b, n = j % 2, PE_TAPS[j]
            for q in range(n):
                if amid is not None and q == n // 2:
                    amid()
                k = DV_TAPS[j] + q
                eng.matmul(ps[:, 4 + b, :], diagh[b][:, q, :], gluh[:, b, k:k + SEQ], start=(q == 0), stop=False)
                eng.matmul(ps[:, 4 + b, :], diagh[b][:, q, :], glul[:, b, k:k + SEQ], start=False, stop=False)
                mm = eng.matmul(ps[:, 4 + b, :], diagl[b][:, q, :], gluh[:, b, k:k + SEQ], start=False, stop=(q == n - 1))
            mm.then_inc(dw_pe, 1)

        def to_tm(j):
            eng.wait_ge(conv_c, j + 1)
            if j >= 2:
                eng.wait_ge(ct_ok, j - 1)
            for t in range(NT):
                mm = eng.transpose(ps[:, 6 + j % 2, t * P:(t + 1) * P], cbuf[:, j % 2, t * P:(t + 1) * P], ident[:, :])
            mm.then_inc(ct_pe, 1)

        def busy(n, bank):
            for _ in range(n):
                eng.transpose(ps[:, bank, 0:P], ident[:, :], ident[:, :])

        eng.wait_ge(const_ok, 3)
        busy(26, 7)
        first_units()
        for j in range(1, KD):
            unit_conv(2 * j)
            if j in (1, KD - 1):
                unit_conv(2 * j + 1)
            if j >= 2:
                to_tm(j - 2)
            taps(j - 1)
            if 1 < j < KD - 1:
                unit_conv(2 * j + 1)
        taps(KD - 1, lambda: to_tm(KD - 2))
        to_tm(KD - 1)
        busy(32, 0)

        def to_fm(k):
            if k in ZC_PARTS:
                eng.wait_ge(zc, NT * (ZC_PARTS.index(k) + 1))
            if k >= 2:
                eng.wait_ge(sl, k - 1)
            for t in range(NT):
                mm = eng.transpose(ps[:, 4 + k % 2, t * P:(t + 1) * P], ctm[:, t, k * P:(k + 1) * P], ident[:, :])
            mm.then_inc(zt, 1)

        def conv_tile(k):
            if k == 0:
                to_fm(0)
                to_fm(1)
                busy(12, 0)
            elif k + 1 < KD:
                to_fm(k + 1)
            eng.wait_ge(x_lo, X0 + k + 1)

        def block_fm(n, t):
            eng.wait_ge(x_ok, n * NT + t + 1)
            for q in range(2):
                if t >= 2:
                    eng.wait_ge(x_lo, XC + n * 2 * NT + 2 * (t - 2) + q + 1)
                elif t == 0 and q == 0:
                    eng.wait_ge(mean_ok, n * NT + 1)
                for k in range(4):
                    mm = eng.transpose(ps[:, B0[n] + 2 * (t % 2) + q, k * P:(k + 1) * P],
                                       res[:, t, (4 * q + k) * P:(4 * q + k + 1) * P], ident[:, :])
                mm.then_inc(xt, 1)

        def after(n):
            def f(t):
                if t > 0 and n < 3:
                    block_fm(n, t - 1)
            return f

        def wait_x(n, t):
            eng.wait_ge(x_lo, XC + n * 2 * NT + 2 * (t + 1))

        down_by_k(U_CONV_OUT, 4, 0, xh, xl, 0, KD, conv_tile)
        down_by_block(U_CONV_OUT + 4, 4, 4, xh, xl, 0, KD, after(0))

        def ffn(layer, n, u_up, u_down):
            mid = SEQ // 2
            wait_x(n - 1, 1)
            for c in range(3):
                if c == 2:
                    block_fm(n - 1, NT - 1)
                eng.wait_ge(w_lo, u_up + c + 1)
                up(split_at(u_up + c), B1[n - 1] + c, slice(0, mid))
            wait_x(n - 1, NT - 1)
            for c in range(4):
                eng.wait_ge(w_lo, u_up + c + 1)
                up(split_at(u_up + c), B1[n - 1] + c, slice(mid if c < 3 else 0, SEQ)).then_inc(w_used, 1)
            slot0 = IN_RING.index(u_up + RING) % RING
            with eng.Fori(1, KH // 2) as i:
                for c in range(4):
                    eng.wait_ge(w_lo, i * 4 + (u_up + c + 1))
                    eng.wait_ge(tap, i * 12 + (PAD_TAPS * layer + 6 * KH * layer + 3 * c + 1))
                    slot = (slot0 + c) % RING
                    up((wh[:, slot, :], wl[:, slot, :]), B1[n - 1] + c).then_inc(w_used, 1)

            def hidden(k):
                eng.wait_ge(h_lo, layer * KH + k + 1)
            down_by_k(u_down, KH // 2, B0[n], hh, hl, 0, KH, hidden)
            down_by_k(u_down + KH // 2, KH // 2 - LAST, B1[n], hh, hl, 0, KH)
            down_by_block(u_down + KH - LAST, LAST, B1[n], hh, hl, KH - 2 * LAST, KH, after(n))

        ffn(0, 1, U_UP0, U_DOWN0)

        def last_block(t):
            if t == 0:
                block_fm(1, NT - 1)
        down_by_block(U_GV, 4, 4, xh, xl, 0, KD, last_block, lambda t: wait_x(1, t))
        down_by_k(U_GV + 4, 4, 0, xh, xl, 0, KD)

        def spatial(g):
            if g == 0:
                eng.wait_ge(ws_lo, 1)
                eng.wait_ge(v_lo, NT)
            if g >= 4:
                eng.wait_ge(us_s, g - 3)
            for n in range(NT):
                o = ps[:, g % 4, n * P:(n + 1) * P]
                a, b = vh[:, n, g * P:(g + 1) * P], vl[:, n, g * P:(g + 1) * P]
                eng.matmul(o, a, wsh[:, g, :], start=True, stop=False)
                eng.matmul(o, a, wsl[:, g, :], start=False, stop=False)
                mm = eng.matmul(o, b, wsh[:, g, :], start=False, stop=True)
            mm.then_inc(sp, 1)

        for j in range(KD):
            eng.wait_ge(w_lo, U_GU + j + 1)
            if j < 4:
                eng.wait_ge(v_ev, j + 1)
            else:
                eng.wait_ge(u_gelu, j - 3)
            up(split_at(U_GU + j), 4 + j % 4).then_inc(w_used, 1)
            if j >= KD - 2:
                spatial(2 * (j - KD + 2))
                spatial(2 * (j - KD + 2) + 1)

        def gated(k):
            if k == 0:
                eng.wait_ge(u_gelu, KD)
            eng.wait_ge(us_lo, k + 1)
            if k + 4 < GROUPS:
                spatial(k + 4)

        down_by_k(U_GOUT, 4, 4, xh, xl, 0, KD, gated)
        down_by_block(U_GOUT + 4, 4, 0, xh, xl, 0, KD, after(2))
        ffn(1, 3, U_UP1, U_DOWN1)

    block.__exit__(None, None, None)


def kernel(**inputs):
    import numpy as np
    import concourse.bacc as bacc
    from concourse.bass_utils import run_bass_kernel_spmd

    a = {k: np.asarray(v) for k, v in inputs.items()}

    def up_units(w):
        return w.reshape(KD, P, -1, P).transpose(2, 1, 0, 3).reshape(-1, P, UNIT)

    def down_units(w):
        return w.reshape(-1, 2, P, 2, HALF).transpose(3, 0, 2, 1, 4).reshape(-1, P, UNIT)

    def interleaved(first, second):
        return np.stack([up_units(first), up_units(second)], 1).reshape(-1, P, UNIT)

    cin, gin = a["conv_w_in"][0], a["gmlp_w_in"][0]
    units = [interleaved(cin[:, D:], cin[:, :D]), down_units(a["conv_w_out"][0])]
    for layer in range(DEPTH):
        w = a["ffn_w_up"][layer]
        if layer == 1:
            units += [down_units(gin[:, D:]), up_units(gin[:, :D]), down_units(a["gmlp_w_out"][0])]
        units += [interleaved(w[:, :HID], w[:, HID:]), down_units(a["ffn_w_down"][layer])]
    weights = np.ascontiguousarray(np.concatenate(units))

    def columns(v):
        return v.reshape(-1, P).T

    def pairs(v):
        v = v.reshape(DEPTH, -1, 2, KH, P)
        return v.transpose(4, 0, 3, 2, 1).reshape(P, -1)

    dw = a["conv_w_dw"][0].reshape(TAPS, KD, P).transpose(2, 1, 0).reshape(P, -1)
    params = np.ascontiguousarray(np.concatenate([
        columns(a["conv_b_in"][0]), dw, columns(a["conv_b_dw"][0]), columns(a["conv_ln_g"][0]),
        columns(a["conv_ln_b"][0]), columns(a["gmlp_b_in"][0][:D]), pairs(a["ffn_b_up"]),
        pairs(a["ffn_w_dw"]), pairs(a["ffn_b_dw"])], 1))
    n1g, n1b, n2g, n2b = a["norm1_g"], a["norm1_b"], a["norm2_g"], a["norm2_b"]
    rows = np.ascontiguousarray(np.stack([
        n1g[0], n1b[0], n2g[0], n2b[0], n1g[1], n1b[1], n2g[1], n2b[1],
        a["conv_b_out"][0], a["ffn_b_down"][0], a["gmlp_b_out"][0], a["ffn_b_down"][1],
        a["gmlp_b_in"][0][D:], a["gmlp_ln_g"][0], a["gmlp_ln_b"][0], a["gmlp_b_s"][0].reshape(-1)]))
    x = a["x"].reshape(SEQ, D)
    arrays = {
        "d_x_tm": np.ascontiguousarray(x),
        "d_x_fm": np.ascontiguousarray(x.reshape(SEQ, KD, P).transpose(2, 1, 0)),
        "d_weights": weights,
        "d_params": params,
        "d_rows": rows,
        "d_spatial": np.ascontiguousarray(a["gmlp_w_s"][0].transpose(2, 0, 1)),
    }
    nc = bacc.Bacc("TRN2", target_bir_lowering=False, num_devices=1)
    args = [nc.dram_tensor(k, v.shape, mybir.dt.from_np(v.dtype), kind="ExternalInput").ap() for k, v in arrays.items()]
    out = nc.dram_tensor("d_out", (SEQ, D), mybir.dt.float32, kind="ExternalOutput").ap()
    build_trunk(nc, *args, out)
    r = run_bass_kernel_spmd(nc, [arrays], core_ids=[0])
    return r.results[0]["d_out"].reshape(1, SEQ, D)
```
